# Optimizing a Trainium2 kernel written in Bass

```python
import jax, jax.numpy as jnp
from jax import lax
import numpy as np

D_MODEL = 1024
BATCH = 1
SEQ = 256
DEPTH = 2

PLE_DIM = 256
D_FF = ((8 * D_MODEL // 3 + 127) // 128) * 128
CONV_CH = D_MODEL
CONV_K = 31
RET_HEADS = 4
RET_QK_DIM = D_MODEL // RET_HEADS
RET_V_DIM = 2 * D_MODEL // RET_HEADS
RET_QK = RET_HEADS * RET_QK_DIM
RET_V = RET_HEADS * RET_V_DIM
CHUNK = 128
ROPE_BASE = 10000.0
EPS = 1e-6
IN_W = 2 * CONV_CH + 2 * RET_QK + 2 * RET_V + 2 * D_MODEL

kernel_name = "hybrid_conformer_conv_retention_gated_macaron"

def rms_norm(t, g):
    tf = t.astype(jnp.float32)
    y = tf * lax.rsqrt(jnp.mean(tf * tf, axis=-1, keepdims=True) + EPS)
    return (y * g.astype(jnp.float32)).astype(t.dtype)

def layer_norm(t, g, b):
    tf = t.astype(jnp.float32)
    mu = jnp.mean(tf, axis=-1, keepdims=True)
    var = jnp.mean(jnp.square(tf - mu), axis=-1, keepdims=True)
    y = (tf - mu) * lax.rsqrt(var + EPS)
    return (y * g.astype(jnp.float32) + b.astype(jnp.float32)).astype(t.dtype)

def swiglu(t, w_gate, w_up, w_down):
    return (jax.nn.silu(t @ w_gate) * (t @ w_up)) @ w_down

def rotary(t, positions):
    half = t.shape[-1] // 2
    inv = ROPE_BASE ** (-jnp.arange(half, dtype=jnp.float32) / half)
    ang = positions.astype(jnp.float32)[..., None] * inv
    cos = jnp.cos(ang)[:, :, None, :]
    sin = jnp.sin(ang)[:, :, None, :]
    t1 = t[..., :half].astype(jnp.float32)
    t2 = t[..., half:].astype(jnp.float32)
    return jnp.concatenate([t1 * cos - t2 * sin, t2 * cos + t1 * sin], axis=-1).astype(t.dtype)

def conv_module(a, w_dw, b_dw, ln_g, ln_b, w_o):
    glu = a[..., :CONV_CH] * jax.nn.sigmoid(a[..., CONV_CH:])
    y = lax.conv_general_dilated(
        glu, w_dw[:, None, :].astype(glu.dtype), window_strides=(1,),
        padding=[(CONV_K - 1, 0)], dimension_numbers=("NWC", "WIO", "NWC"),
        feature_group_count=CONV_CH) + b_dw
    y = layer_norm(y, ln_g, ln_b)
    return jax.nn.silu(y) @ w_o

def retention(q, k, v):
    B, S, H, dk = q.shape
    dv = v.shape[-1]
    n = S // CHUNK
    log_g = jnp.log1p(-jnp.exp2(-5.0 - jnp.arange(H, dtype=jnp.float32)))
    idx = jnp.arange(CHUNK, dtype=jnp.float32)
    rel = idx[:, None] - idx[None, :]
    intra = jnp.where(rel >= 0, jnp.exp(log_g[:, None, None] * jnp.maximum(rel, 0.0)), 0.0)
    q_dec = jnp.exp(log_g[:, None] * (idx + 1.0))
    k_dec = jnp.exp(log_g[:, None] * (CHUNK - 1.0 - idx))
    chunk_dec = jnp.exp(log_g * CHUNK)

    def to_chunks(t):
        return t.astype(jnp.float32).reshape(B, n, CHUNK, H, t.shape[-1]).transpose(1, 0, 3, 2, 4)

    qc = to_chunks(q)
    kc = to_chunks(k) * (dk ** -0.5)
    vc = to_chunks(v)

    def step(state, qkv):
        qb, kb, vb = qkv
        scores = jnp.einsum("bhid,bhjd->bhij", qb, kb) * intra
        inner = jnp.einsum("bhij,bhje->bhie", scores, vb)
        cross = jnp.einsum("bhid,bhde->bhie", qb * q_dec[..., None], state)
        state = chunk_dec[:, None, None] * state + jnp.einsum(
            "bhjd,bhje->bhde", kb * k_dec[..., None], vb)
        return state, inner + cross

    s0 = jnp.zeros((B, H, dk, dv), jnp.float32)
    _, out = lax.scan(step, s0, (qc, kc, vc))
    return out.transpose(1, 0, 3, 2, 4).reshape(B, S, H, dv)

def setup_inputs(seed: int = 0) -> dict:
    key = jax.random.key(seed)
    ks = iter(jax.random.split(key, 40))

    def w(shape, fan_in):
        return jax.random.normal(next(ks), shape, jnp.float32) * (fan_in ** -0.5)

    def gain(shape):
        return 1.0 + 0.02 * jax.random.normal(next(ks), shape, jnp.float32)

    def small(shape):
        return 0.02 * jax.random.normal(next(ks), shape, jnp.float32)

    x = jax.random.normal(next(ks), (BATCH, SEQ, D_MODEL), jnp.float32)
    p = jax.random.normal(next(ks), (DEPTH, BATCH, SEQ, PLE_DIM), jnp.float32)
    offset = jax.random.randint(next(ks), (BATCH, 1), 0, 1024, dtype=jnp.int32)
    positions = offset + jnp.arange(SEQ, dtype=jnp.int32)[None, :]
    return {
        "x": x, "p": p, "positions": positions,
        "ffn1_norm": gain((DEPTH, D_MODEL)),
        "ffn1_w_gate": w((DEPTH, D_MODEL, D_FF), D_MODEL),
        "ffn1_w_up": w((DEPTH, D_MODEL, D_FF), D_MODEL),
        "ffn1_w_down": w((DEPTH, D_FF, D_MODEL), D_FF),
        "mix_norm": gain((DEPTH, D_MODEL)),
        "w_in": w((DEPTH, D_MODEL, IN_W), D_MODEL),
        "b_gates": small((DEPTH, 2, D_MODEL)),
        "conv_w": w((DEPTH, CONV_K, CONV_CH), CONV_K),
        "conv_b": small((DEPTH, CONV_CH)),
        "conv_ln_g": gain((DEPTH, CONV_CH)),
        "conv_ln_b": small((DEPTH, CONV_CH)),
        "w_conv_o": w((DEPTH, CONV_CH, D_MODEL), CONV_CH),
        "w_ret_o": w((DEPTH, RET_V, D_MODEL), RET_V),
        "w_out": w((DEPTH, D_MODEL, D_MODEL), D_MODEL),
        "ffn2_norm": gain((DEPTH, D_MODEL)),
        "ffn2_w_gate": w((DEPTH, D_MODEL, D_FF), D_MODEL),
        "ffn2_w_up": w((DEPTH, D_MODEL, D_FF), D_MODEL),
        "ffn2_w_down": w((DEPTH, D_FF, D_MODEL), D_FF),
        "ple_norm": gain((DEPTH, D_MODEL)),
        "w_ple_gate": w((DEPTH, D_MODEL, D_MODEL), D_MODEL),
        "w_ple_proj": w((DEPTH, PLE_DIM, D_MODEL), PLE_DIM),
        "ple_proj_norm": gain((DEPTH, D_MODEL)),
        "final_norm": gain((D_MODEL,)),
    }

def reference(x, p, positions, ffn1_norm, ffn1_w_gate, ffn1_w_up, ffn1_w_down,
              mix_norm, w_in, b_gates, conv_w, conv_b, conv_ln_g, conv_ln_b,
              w_conv_o, w_ret_o, w_out, ffn2_norm, ffn2_w_gate, ffn2_w_up, ffn2_w_down,
              ple_norm, w_ple_gate, w_ple_proj, ple_proj_norm, final_norm):
    B, S, _ = x.shape
    split_idx = np.cumsum([2 * CONV_CH, RET_QK, RET_QK, RET_V, RET_V, D_MODEL]).tolist()
    h = x
    for i in range(DEPTH):
        h = h + 0.5 * swiglu(rms_norm(h, ffn1_norm[i]), ffn1_w_gate[i], ffn1_w_up[i], ffn1_w_down[i])

        u = rms_norm(h, mix_norm[i])
        z = u @ w_in[i]
        a_conv, q, k, v, g_ret, z_ga, z_gb = jnp.split(z, split_idx, axis=-1)

        y_a = conv_module(a_conv, conv_w[i], conv_b[i], conv_ln_g[i], conv_ln_b[i], w_conv_o[i])

        qh = rotary(q.reshape(B, S, RET_HEADS, RET_QK_DIM), positions)
        kh = rotary(k.reshape(B, S, RET_HEADS, RET_QK_DIM), positions)
        o = retention(qh, kh, v.reshape(B, S, RET_HEADS, RET_V_DIM))
        o = o * lax.rsqrt(jnp.mean(o * o, axis=-1, keepdims=True) + EPS)
        o = (jax.nn.silu(g_ret.astype(jnp.float32)) * o.reshape(B, S, RET_V)).astype(h.dtype)
        y_b = o @ w_ret_o[i]

        m = jax.nn.sigmoid(z_ga + b_gates[i, 0]) * y_a + jax.nn.sigmoid(z_gb + b_gates[i, 1]) * y_b
        h = h + m @ w_out[i]

        h = h + 0.5 * swiglu(rms_norm(h, ffn2_norm[i]), ffn2_w_gate[i], ffn2_w_up[i], ffn2_w_down[i])

        e = rms_norm(p[i].astype(h.dtype) @ w_ple_proj[i], ple_proj_norm[i])
        gate = jax.nn.sigmoid(rms_norm(h, ple_norm[i]) @ w_ple_gate[i])
        h = h + gate * e
    return rms_norm(h, final_norm)


_drawn_inputs = setup_inputs


def setup_inputs(seed=0):
    import zlib

    import numpy as np

    out = dict(_drawn_inputs(seed))
    spreads = {}
    factors = {'ffn1_norm': 4.964,
     'mix_norm': 9.121,
     'b_gates': 8.0,
     'conv_b': 8.697,
     'conv_ln_g': 32.758,
     'conv_ln_b': 32.885,
     'ffn2_norm': 6.117,
     'ple_norm': 64.0,
     'ple_proj_norm': 39.648,
     'final_norm': 7.866}
    for name, (base, spread) in spreads.items():
        noise = np.random.default_rng([zlib.crc32(name.encode()), seed]).standard_normal(out[name].shape)
        drawn = base * np.exp(spread * noise) if base else spread * noise
        out[name] = __import__('jax').numpy.asarray(drawn.astype(out[name].dtype))
    for name, factor in factors.items():
        out[name] = (out[name] * factor).astype(out[name].dtype)
    return out
```

```python
from contextlib import ExitStack

import numpy as np

import concourse.bass as bass
from concourse import mybir

ALU = mybir.AluOpType
ACT = mybir.ActivationFunctionType
F32 = mybir.dt.float32
F32R = mybir.dt.float32r
I32 = mybir.dt.int32

P = 128
DEPTH = 2
D = 1024
SEQ = 256
TB = SEQ // P
KT = D // P
D_FF = ((8 * D // 3 + 127) // 128) * 128
PLE = 256
CONV_K = 31
HEADS = 4
DK = D // HEADS
DV = 2 * D // HEADS
EPS = 1e-6
ROPE_BASE = 10000.0
HALF = DK // 2
COLS = 512
CHUNK = 2048
SLOTS = 3
FFN_UNITS = D_FF // 256

FFN1 = 0
FFN_CHUNKS = 3 * FFN_UNITS
WIN = FFN1 + FFN_CHUNKS
WIN_UNITS = 20
RET = WIN + 2 * WIN_UNITS
CONVO = RET + 2 * HEADS
OUT = CONVO + 4
PLEP = OUT + 4
FFN2 = PLEP + 1
PG = FFN2 + FFN_CHUNKS
LAYER = PG + 4
USES = [(LAYER - s + SLOTS - 1) // SLOTS for s in range(SLOTS)]

U_CONV, U_GATE, U_QK, U_V, U_G = 0, 4, 8, 12, 16

V_FFN1, V_MIX, V_FFN2, V_PLE, V_CONVB, V_LNG, V_LNB, V_TAPS = 0, 1, 2, 3, 4, 5, 6, 7
NVEC = 7 + CONV_K

N_FFN1, N_MIX, N_FFN2, N_PLE = range(4)

MAGIC = 12582912.0
TWO_PI = 6.283185307179586
C1 = 6.28125
C2 = float(np.float32(TWO_PI - C1) - np.float32(np.float32(TWO_PI - C1) % np.float32(2.0 ** -20)))
C3 = TWO_PI - C1 - C2

PI_IN = 3.1415925
ROPE_STEPS = 17
POOL_STEPS = 14
CONV_STEPS = 9


def slot(c):
    return c % SLOTS


def nth(c, layer, j=0):
    return layer * USES[c % SLOTS] + c // SLOTS + j


def build_kernel(nc, stream, x, p, positions, vectors, b_gates, ple_gain, final_gain,
                 decay, inv_freq, identity, mean_matrix, out):
    ctx = ExitStack()
    with ctx:
        def sem(name):
            return ctx.enter_context(nc.semaphore(name))

        top = [-(-nc.sbuf_base // 32) * 32]

        def at(name, shape, dt=F32, offset=None):
            n = 4 * int(np.prod(shape[1:]))
            o = top[0] if offset is None else offset
            if offset is None:
                top[0] += n
            return nc.alloc_sbuf_tensor_at(name, shape, dt, offset=o), o

        raw, _ = at("raw", [P, SLOTS, CHUNK])
        w_hi, _ = at("w_hi", [P, SLOTS, CHUNK], F32R)
        w_lo, _ = at("w_lo", [P, SLOTS, CHUNK], F32R)
        h, _ = at("h", [P, TB, D])
        uT_hi, _ = at("uT_hi", [P, KT, SEQ], F32R)
        uT_lo, o_uT_lo = at("uT_lo", [P, KT, SEQ], F32R)
        centred_sq, _ = at("centred_sq", [P, KT, SEQ], offset=o_uT_lo)
        gate_a, _ = at("gate_a", [P, TB, D])
        gate_b, _ = at("gate_b", [P, TB, D])
        v, o_v = at("v", [P, TB, HEADS * DV])
        mT_hi, _ = at("mT_hi", [P, KT, SEQ], F32R, offset=o_v)
        mT_lo, _ = at("mT_lo", [P, KT, SEQ], F32R, offset=o_v + 8192)
        swish_g, o_sg = at("swish_g", [P, TB, HEADS * DV])
        gate_bias, _ = at("gate_bias", [P, 2 * D], offset=o_sg)
        roped, _ = at("roped", [P, TB, 2, 2, HALF], offset=o_sg)
        prod_a, _ = at("prod_a", [P, TB, 2, HALF], offset=o_sg + 4096)
        prod_b, _ = at("prod_b", [P, TB, 2, HALF], offset=o_sg + 6144)
        qk_in, _ = at("qk_in", [P, 2, TB, 2, 2, HALF], offset=o_sg + 8192)
        qT, o_qT = at("qT", [P, KT, SEQ])
        kT, o_kT = at("kT", [P, KT, SEQ])
        e_buf, _ = at("e_buf", [P, TB, D], offset=o_qT)
        gain_e, _ = at("gain_e", [P, D], offset=o_kT)
        gain_f, _ = at("gain_f", [P, D], offset=o_kT + 4096)
        PAD = CONV_K - 1
        gluT, _ = at("gluT", [P, KT, PAD + SEQ])
        yT, o_yT = at("yT", [P, KT, SEQ])
        p_in, _ = at("p_in", [P, TB, PLE], offset=o_yT)
        hT_hi, _ = at("hT_hi", [P, 4, SEQ], F32R)
        hT_lo, _ = at("hT_lo", [P, 4, SEQ], F32R)
        scaled, _ = at("scaled", [P, 2, 4 * P])
        acted, _ = at("acted", [P, TB, 256])
        mid, _ = at("mid", [P, TB, 256])
        junk, _ = at("junk", [P, COLS])
        scores, _ = at("scores", [P, 3 * P])
        decay_sb, _ = at("decay_sb", [P, HEADS, SEQ])
        cos_sb, _ = at("cos_sb", [P, TB, HALF])
        sin_sb, _ = at("sin_sb", [P, TB, HALF])
        ident, _ = at("ident", [P, P])
        means, _ = at("means", [P, P])
        vec, _ = at("vec", [P, NVEC, KT])
        vec_ple, _ = at("vec_ple", [P, KT])
        small, _ = at("small", [P, 64])
        x_in, _ = at("x_in", [P, TB, D], offset=o_qT)
        angle, _ = at("angle", [P, TB, HALF], offset=o_v)
        turns, _ = at("turns", [P, TB, HALF], offset=o_v + 1024)
        turns_c, _ = at("turns_c", [P, TB, HALF], offset=o_v + 2048)
        inv_sb, _ = at("inv_sb", [P, HALF], offset=o_v + 3072)
        pos_i, _ = at("pos_i", [P, TB], I32, offset=o_v + 4096)
        pos_f, _ = at("pos_f", [P, TB], offset=o_v + 4128)
        assert top[0] <= nc.sbuf_usable_end, top[0]

        ssq = small[:, 0:4].rearrange("p (t n) -> p t n", t=TB)
        ms = small[:, 4:6]
        rstd = small[:, 6:8]
        ssq_head = small[:, 8:10]
        ms_head = small[:, 10:12]
        r_head = small[:, 12:14]
        ssq_e = small[:, 14:18].rearrange("p (t n) -> p t n", t=TB)
        ms_e = small[:, 18:20]
        r_e = small[:, 20:22]
        minus_half = small[:, 22:24]
        eps_tile = small[:, 28:30]
        ssq_sum = small[:, 24:26]
        ssq_e_sum = small[:, 26:28]

        ps = ctx.enter_context(nc.psum_tensor("ps", [P, 8, COLS], F32))
        T0, T1 = 6, 7

        landed = [sem(f"landed{s}") for s in range(SLOTS)]
        hi_done = [sem(f"hi_done{s}") for s in range(SLOTS)]
        lo_done = [sem(f"lo_done{s}") for s in range(SLOTS)]
        used = [sem(f"used{s}") for s in range(SLOTS)]
        tb0_done = sem("tb0_done")
        piece_done = sem("piece_done")
        h_ready = sem("h_ready")
        norm_T = sem("norm_T")
        norm_g = sem("norm_g")
        norm_hi = sem("norm_hi")
        norm_lo = sem("norm_lo")
        ssq_ready = sem("ssq_ready")
        rstd_ready = sem("rstd_ready")
        acted_ready = sem("acted_ready")
        mid_ready = sem("mid_ready")
        mid_T = sem("mid_T")
        mid_hi = sem("mid_hi")
        mid_lo = sem("mid_lo")
        unit_act = sem("unit_act")
        gate_pre = sem("gate_pre")
        gate_act = sem("gate_act")
        roped_ready = sem("roped_ready")
        rope_step = sem("rope_step")
        qk_T = sem("qk_T")
        qk_evac = sem("qk_evac")
        conv_step = sem("conv_step")
        mean_done = sem("mean_done")
        centred = sem("centred")
        squared = sem("squared")
        var_eps = sem("var_eps")
        std_ready = sem("std_ready")
        ln_rstd = sem("ln_rstd")
        normed = sem("normed")
        ln_silu = sem("ln_silu")
        ln_hi = sem("ln_hi")
        convT_lo = sem("convT_lo")
        score_done = sem("score_done")
        decayed = sem("decayed")
        pv_done = sem("pv_done")
        head_ssq = sem("head_ssq")
        head_r = sem("head_r")
        head_ready = sem("head_ready")
        head_T = sem("head_T")
        head_hi = sem("head_hi")
        head_lo = sem("head_lo")
        ret_gated = sem("ret_gated")
        conv_gated = sem("conv_gated")
        m_ready = sem("m_ready")
        m_T = sem("m_T")
        m_hi = sem("m_hi")
        m_lo = sem("m_lo")
        p_T = sem("p_T")
        p_hi = sem("p_hi")
        p_lo = sem("p_lo")
        e_squared = sem("e_squared")
        e_evac = sem("e_evac")
        e_r = sem("e_r")
        e_normed = sem("e_normed")
        pg_act = sem("pg_act")
        pg_prod = sem("pg_prod")
        pool_step = sem("pool_step")
        consts = sem("consts")
        rope_in = sem("rope_in")
        x_landed = sem("x_landed")
        vec_landed = sem("vec_landed")
        ple_landed = sem("ple_landed")
        bias_landed = sem("bias_landed")
        p_landed = sem("p_landed")
        gain_landed = sem("gain_landed")
        start_step = sem("start_step")
        trig = sem("trig")
        preset = sem("preset")
        out_ready = sem("out_ready")
        stored = sem("stored")

        def half_of(i):
            return i // TB, i % TB

        def cols(n):
            return slice(n * COLS, (n + 1) * COLS)

        def toks(t):
            return slice(t * P, (t + 1) * P)

        block = ctx.enter_context(nc.Block())

        @block.sync
        def _(sp):
            def load(c, layer, j=0):
                sp.wait_ge(lo_done[slot(c)], nth(c, layer, j) + 1)
                sp.dma_start(raw[:, slot(c), :],
                             stream[bass.ds(layer * LAYER + c + SLOTS * j, 1), :, :].rearrange("a p n -> p (a n)")
                             ).then_inc(landed[slot(c)], 16)

            groups = LAYER // SLOTS
            with sp.Fori(0, DEPTH) as layer:
                with sp.Fori(0, groups) as j:
                    for c in range(SLOTS):
                        load(c, layer, j)
                for c in range(groups * SLOTS, LAYER):
                    load(c, layer)
            sp.wait_ge(out_ready, TB)
            sp.dma_start(out.rearrange("b (t p) d -> p (b t) d", p=P), e_buf[:, :, :]).then_inc(stored, 16)
            sp.wait_ge(stored, 16)

        @block.tensor
        def _(pe):
            def product(bank, lhs_hi, lhs_lo, kts, t, c, first, last, col=None):
                s = slot(c)
                steps = []
                for i, kt in enumerate(kts):
                    rows = slice(i * COLS, (i + 1) * COLS) if col is None else slice(i * D + col, i * D + col + COLS)
                    for a, b in ((lhs_hi, w_hi), (lhs_hi, w_lo), (lhs_lo, w_hi)):
                        steps.append((a[:, kt, toks(t)], b[:, s, rows]))
                for n, (a, b) in enumerate(steps):
                    mm = pe.matmul(ps[:, bank, :], a, b, start=first and n == 0, stop=last and n == len(steps) - 1)
                return mm

            def half_unit(c, layer, banks, lhs_hi, lhs_lo, second, j=0):
                pe.wait_ge(lo_done[slot(c)], nth(c, layer, j) + 2)
                kts = range(4, 8) if second else range(4)
                mm = product(banks[0], lhs_hi, lhs_lo, kts, 0, c, not second, second)
                if second:
                    mm.then_inc(tb0_done, 1)
                product(banks[1], lhs_hi, lhs_lo, kts, 1, c, not second, second).then_inc(used[slot(c)], 1)

            def rows_chunk(c, layer, lhs_hi, lhs_lo, kts, first, last, banks=(0, 1, 2, 3), j=0, pieces=True):
                pe.wait_ge(lo_done[slot(c)], nth(c, layer, j) + 2)
                for i in range(4):
                    n, t = half_of(i)
                    mm = product(banks[i], lhs_hi, lhs_lo, kts, t, c, first, last, col=n * COLS)
                    if i == 3:
                        mm.then_inc(used[slot(c)], 1)
                    elif last:
                        mm.then_inc(piece_done, 1)

            def transpose4(bank, pieces):
                for n, a in enumerate(pieces):
                    mm = pe.transpose(ps[:, bank, n * P:(n + 1) * P], a, ident[:, :])
                return mm

            def norm_transposes(layer, q, pieces=range(4)):
                for i in pieces:
                    n, t = half_of(i)
                    pe.wait_ge(h_ready, layer * 16 + q * 4 + i + 1)
                    if i >= 2:
                        pe.wait_ge(norm_g, layer * 16 + q * 4 + i - 1)
                    transpose4(T0 + i % 2, [h[:, t, n * COLS + k * P:n * COLS + (k + 1) * P] for k in range(4)]
                               ).then_inc(norm_T, 1)

            def norm_ready(layer, q, second):
                pe.wait_ge(norm_lo, layer * 16 + q * 4 + (4 if second else 2))

            def mid_transposes(layer, n):
                pe.wait_ge(mid_ready, layer * 52 + 2 * n + 2)
                transpose4(T0, [mid[:, t, k * P:(k + 1) * P] for k in range(2) for t in range(TB)]
                           ).then_inc(mid_T, 1)

            def ffn(layer, F, q, mids):
                def down(c, j, first=False, last=False, unit=0):
                    pe.wait_ge(mid_lo, layer * 22 + (11 if F else 0) + unit + j + 1)
                    rows_chunk(c, layer, hT_hi, hT_lo, range(2), first, last, j=j)

                norm_ready(layer, q, False)
                half_unit(F, layer, (4, 5), uT_hi, uT_lo, False)
                norm_ready(layer, q, True)
                half_unit(F + 1, layer, (4, 5), uT_hi, uT_lo, True)
                mid_transposes(layer, mids)

                def unit(j, first=False):
                    half_unit(F + 2, layer, (4, 5), uT_hi, uT_lo, False, j=j)
                    half_unit(F + 3, layer, (4, 5), uT_hi, uT_lo, True, j=j)
                    if first and F:
                        pe.wait_ge(e_evac, layer * 4 + 4)
                    down(F + 4, j, first=first)
                    mid_transposes(layer, mids + 1 + j)

                unit(0, first=True)
                with pe.Fori(1, FFN_UNITS - 1) as j:
                    unit(j)
                down(F + FFN_CHUNKS - 1, 0, last=True, unit=FFN_UNITS - 1)

            def head_scores(layer, hd):
                pe.wait_ge(qk_evac, layer * 8 + 8)
                for k in range(2):
                    pe.matmul(ps[:, T0, 0:SEQ], kT[:, 2 * hd + k, 0:P], qT[:, 2 * hd + k, :],
                              start=k == 0, stop=k == 1)
                for k in range(2):
                    mm = pe.matmul(ps[:, T0, SEQ:SEQ + P], kT[:, 2 * hd + k, P:SEQ], qT[:, 2 * hd + k, P:SEQ],
                                   start=k == 0, stop=k == 1)
                mm.then_inc(score_done, 1)

            def head_values(layer, hd):
                pe.wait_ge(decayed, layer * HEADS + hd + 1)
                cv = slice(hd * DV, (hd + 1) * DV)
                pe.matmul(ps[:, 4, :], scores[:, 0:P], v[:, 0, cv], start=True, stop=True).then_inc(pv_done, 1)
                pe.matmul(ps[:, 5, :], scores[:, P:SEQ], v[:, 0, cv], start=True, stop=False)
                pe.matmul(ps[:, 5, :], scores[:, SEQ:3 * P], v[:, 1, cv], start=False, stop=True).then_inc(pv_done, 1)

            def head_transposes(layer, hd):
                for t in range(TB):
                    pe.wait_ge(head_ready, layer * 8 + 2 * hd + t + 1)
                    transpose4(T1 - t, [scaled[:, t, k * P:(k + 1) * P] for k in range(4)]).then_inc(head_T, 1)

            def m_transposes(layer, pieces):
                for i in pieces:
                    n, t = half_of(i)
                    pe.wait_ge(m_ready, layer * 4 + i + 1)
                    if i >= 2:
                        pe.wait_ge(m_lo, layer * 4 + i - 1)
                    transpose4(T0 + i % 2, [gate_a[:, t, n * COLS + k * P:n * COLS + (k + 1) * P] for k in range(4)]
                               ).then_inc(m_T, 1)

            for s in range(SLOTS):
                pe.sem_inc(used[s], 1)
            pe.wait_ge(consts, 48)
            with pe.Fori(0, DEPTH) as layer:
                norm_transposes(layer, N_FFN1)
                ffn(layer, FFN1, N_FFN1, 0)
                norm_transposes(layer, N_MIX)
                for u in range(WIN_UNITS):
                    banks = (u % 3 * 2, u % 3 * 2 + 1)
                    if u == 0:
                        norm_ready(layer, N_MIX, False)
                    w = u - 3
                    if U_CONV <= w < U_GATE:
                        pe.wait_ge(mid_ready, layer * 52 + 22 + 2 * w + 2)
                    elif U_GATE <= w < U_QK:
                        pe.wait_ge(gate_pre, layer * 8 + 2 * (w - U_GATE) + 2)
                    elif U_QK <= w:
                        pe.wait_ge(unit_act, layer * 24 + 2 * (w - U_QK) + 2)
                    half_unit(WIN + 2 * u, layer, banks, uT_hi, uT_lo, False)
                    if u == 0:
                        norm_ready(layer, N_MIX, True)
                    half_unit(WIN + 2 * u + 1, layer, banks, uT_hi, uT_lo, True)
                    if U_CONV < u <= U_GATE:
                        if u - 1 > U_CONV:
                            pe.wait_ge(mid_hi, layer * 26 + 11 + u - 1)
                        mid_transposes(layer, 11 + u - 1)
                    if U_QK + 2 <= u < U_QK + 6:
                        w = u - 2 - U_QK
                        pe.wait_ge(roped_ready, layer * 4 + w + 1)
                        for t in range(TB):
                            if w:
                                pe.wait_ge(qk_evac, layer * 8 + 2 * (w - 1) + t + 1)
                            transpose4(T0 + t, [roped[:, t, k // 2, k % 2, :] for k in range(4)]).then_inc(qk_T, 1)
                    if u == 17:
                        head_scores(layer, 0)
                    if u == 18:
                        pe.wait_ge(unit_act, layer * 24 + 2 * (17 - U_QK) + 2)
                        head_values(layer, 0)
                    if u == 19:
                        head_transposes(layer, 0)
                pe.wait_ge(unit_act, layer * 24 + 24)
                for hd in range(HEADS):
                    pe.wait_ge(head_lo, layer * 8 + 2 * hd + 2)
                    if hd + 1 < HEADS:
                        head_scores(layer, hd + 1)
                    if hd == 1:
                        pe.wait_ge(conv_step, (layer + 1) * CONV_K * KT)
                        for k in range(KT):
                            mm = pe.matmul(ps[:, T1, 0:SEQ], means[:, :], yT[:, k, :], start=k == 0, stop=k == KT - 1)
                        mm.then_inc(mean_done, 1)
                    if hd == 2:
                        pe.wait_ge(squared, layer * 2 + 2)
                        for k in range(KT):
                            mm = pe.matmul(ps[:, T1, 0:SEQ], means[:, :], centred_sq[:, k, :], start=k == 0, stop=k == KT - 1)
                        mm.then_inc(mean_done, 1)
                    rows_chunk(RET + 2 * hd, layer, hT_hi, hT_lo, range(2), hd == 0, False)
                    if hd + 1 < HEADS:
                        head_values(layer, hd + 1)
                    rows_chunk(RET + 2 * hd + 1, layer, hT_hi, hT_lo, range(2, 4), False, hd == HEADS - 1)
                    if hd == 1:
                        pe.wait_ge(centred, layer * 2 + 2)
                    if hd == 2:
                        pe.wait_ge(var_eps, layer + 1)
                    if hd + 1 < HEADS:
                        head_transposes(layer, hd + 1)
                for n in range(2):
                    banks = ((4, 5), (0, 1))[n]
                    if n == 0:
                        pe.wait_ge(convT_lo, layer * 2 + 1)
                    else:
                        pe.wait_ge(ret_gated, layer * 4 + 2)
                    half_unit(CONVO + 2 * n, layer, banks, uT_hi, uT_lo, False)
                    if n == 0:
                        pe.wait_ge(convT_lo, layer * 2 + 2)
                    else:
                        m_transposes(layer, (0, 1))
                    half_unit(CONVO + 2 * n + 1, layer, banks, uT_hi, uT_lo, True)
                m_transposes(layer, (2, 3))
                for n in range(2):
                    banks = ((2, 3), (4, 5))[n]
                    if n == 0:
                        pe.wait_ge(ret_gated, layer * 4 + 4)
                        pe.wait_ge(m_lo, layer * 4 + 2)
                    half_unit(OUT + 2 * n, layer, banks, mT_hi, mT_lo, False)
                    if n == 0:
                        pe.wait_ge(m_lo, layer * 4 + 4)
                    half_unit(OUT + 2 * n + 1, layer, banks, mT_hi, mT_lo, True)
                    if n == 0:
                        pe.wait_ge(p_landed, layer * 16 + 16)
                        transpose4(T0, [p_in[:, t, k * P:(k + 1) * P] for k in range(2) for t in range(TB)]
                                   ).then_inc(p_T, 1)
                pe.wait_ge(p_lo, layer + 1)
                norm_transposes(layer, N_FFN2, (0, 1))
                rows_chunk(PLEP, layer, hT_hi, hT_lo, range(2), True, True)
                norm_transposes(layer, N_FFN2, (2, 3))
                ffn(layer, FFN2, N_FFN2, 15)
                norm_transposes(layer, N_PLE)
                for n in range(2):
                    banks = ((4, 5), (0, 1))[n]
                    if n == 0:
                        norm_ready(layer, N_PLE, False)
                    half_unit(PG + 2 * n, layer, banks, uT_hi, uT_lo, False)
                    if n == 0:
                        norm_ready(layer, N_PLE, True)
                    half_unit(PG + 2 * n + 1, layer, banks, uT_hi, uT_lo, True)

        T_FFN1, T_WIN, T_CONVO, T_OUT, T_FFN2, T_PG, T_LAYER = 0, 11, 31, 33, 35, 46, 48
        P_FFN1, P_RET, P_E, P_FFN2, P_LAYER = 0, 3, 6, 9, 12

        def unit_block(eng, layer, t, first_index, last_chunk, j=0, k=0):
            if t == 0:
                eng.wait_ge(tb0_done, layer * T_LAYER + first_index + k + 1)
            else:
                eng.wait_ge(used[slot(last_chunk)], nth(last_chunk, layer, j) + 2)

        def last_piece(eng, layer, i, first_index, last_chunk):
            if i < 3:
                eng.wait_ge(piece_done, layer * P_LAYER + first_index + i + 1)
            else:
                eng.wait_ge(used[slot(last_chunk)], nth(last_chunk, layer) + 2)

        @block.scalar
        def _(act):
            def split_hi(c, layer, j=0):
                s = slot(c)
                act.wait_ge(landed[s], 16 * (nth(c, layer, j) + 1))
                act.wait_ge(used[s], nth(c, layer, j) + 1)
                act.activation(w_hi[:, s, :], raw[:, s, :], ACT.Copy).then_inc(hi_done[s], 1)

            def norm_his(layer, q, pieces):
                for i in pieces:
                    n, t = half_of(i)
                    act.wait_ge(norm_g, layer * 16 + q * 4 + i + 1)
                    act.activation(uT_hi[:, 4 * n:4 * n + 4, toks(t)],
                                   scaled[:, i % 2, :].rearrange("p (k t) -> p k t", k=4),
                                   ACT.Copy).then_inc(norm_hi, 1)

            def squares(layer, q):
                for t in range(TB):
                    for n in range(2):
                        if t or n:
                            act.wait_ge(ssq_ready, layer * 16 + q * 4 + 2 * t + n)
                        act.activation(junk[:, :], h[:, t, cols(n)], ACT.Square, scale=D ** -0.5,
                                       accum_out=ssq[:, t, n:n + 1]).then_inc(ssq_ready, 1)

            def gated(layer, n, func, first_index, last_chunk, j=0, k=0):
                for t in range(TB):
                    unit_block(act, layer, t, first_index, last_chunk, j, k)
                    act.activation(acted[:, t, :], ps[:, n + t, 0:256], func, scale=rstd[:, t:t + 1]
                                   ).then_inc(acted_ready, 1)

            def ffn(layer, F, q, mids, first_index):
                def mid_upper(k):
                    act.wait_ge(mid_T, layer * 26 + mids + k + 1)
                    act.activation(hT_hi[:, 0:2, :], ps[:, T0, :].rearrange("p (k t) -> p k t", k=2),
                                   ACT.Copy).then_inc(mid_hi, 1)

                split_hi(F + 2, layer)
                act.wait_ge(rstd_ready, layer * 4 + q + 1)
                gated(layer, 4, ACT.Silu, first_index, F + 1)
                split_hi(F + 3, layer)

                def unit(j):
                    mid_upper(j)
                    split_hi(F + 4, layer, j)
                    split_hi(F + 5, layer, j)
                    gated(layer, 4, ACT.Silu, first_index + 1, F + 3, j, j)
                    split_hi(F + 6, layer, j)

                unit(0)
                with act.Fori(1, FFN_UNITS - 1) as j:
                    unit(j)
                mid_upper(FFN_UNITS - 1)
                split_hi(F + FFN_CHUNKS + 1, layer)

            def head_squares(layer, hd):
                for t in range(TB):
                    act.wait_ge(pv_done, layer * 8 + 2 * hd + t + 1)
                    if t:
                        act.wait_ge(head_ssq, layer * 8 + 2 * hd + t)
                    act.activation(junk[:, :], ps[:, 4 + t, :], ACT.Square, scale=DV ** -0.5,
                                   accum_out=ssq_head[:, t:t + 1]).then_inc(head_ssq, 1)

            def head_his(layer, hd):
                for t in range(TB):
                    act.wait_ge(head_T, layer * 8 + 2 * hd + t + 1)
                    act.activation(hT_hi[:, :, toks(t)], ps[:, T1 - t, :].rearrange("p (k t) -> p k t", k=4),
                                   ACT.Copy).then_inc(head_hi, 1)

            def m_his(layer, pieces):
                for i in pieces:
                    n, t = half_of(i)
                    act.wait_ge(m_T, layer * 4 + i + 1)
                    act.activation(mT_hi[:, 4 * n:4 * n + 4, toks(t)],
                                   ps[:, T0 + i % 2, :].rearrange("p (k t) -> p k t", k=4),
                                   ACT.Copy).then_inc(m_hi, 1)

            def glu_copy(layer, w):
                act.wait_ge(mid_T, layer * 26 + 11 + w + 1)
                act.activation(gluT[:, 2 * w:2 * w + 2, PAD:PAD + SEQ],
                               ps[:, T0, :].rearrange("p (k t) -> p k t", k=2), ACT.Copy).then_inc(mid_hi, 1)

            def qk_copy(layer, w):
                dest = qT if w < 2 else kT
                for t in range(TB):
                    act.wait_ge(qk_T, layer * 8 + 2 * w + t + 1)
                    act.activation(dest[:, 4 * (w % 2):4 * (w % 2) + 4, toks(t)],
                                   ps[:, T0 + t, :].rearrange("p (k t) -> p k t", k=4), ACT.Copy).then_inc(qk_evac, 1)

            def win_unit(layer, w):
                bank, last = w % 3 * 2, WIN + 2 * w + 1
                if w < U_GATE:
                    if w:
                        act.wait_ge(mid_ready, layer * 52 + 22 + 2 * w)
                    gated(layer, bank, ACT.Sigmoid, T_WIN + w, last)
                    if w:
                        glu_copy(layer, w - 1)
                elif w < U_QK:
                    g = w - U_GATE
                    dest = gate_a if g < 2 else gate_b
                    if g == 0:
                        glu_copy(layer, U_GATE - 1)
                    act.wait_ge(gate_pre, layer * 8 + 2 * g + 2)
                    act.activation(dest[:, :, cols(g % 2)], dest[:, :, cols(g % 2)], ACT.Sigmoid).then_inc(gate_act, 1)
                elif w < U_V:
                    r = w - U_QK
                    if r >= 2:
                        act.wait_ge(roped_ready, layer * 4 + r - 1)
                    for t in range(TB):
                        unit_block(act, layer, t, T_WIN + w, last)
                        act.activation(qk_in[:, r % 2, t].rearrange("p h a c -> p (h a c)"), ps[:, bank + t, :],
                                       ACT.Copy, scale=rstd[:, t:t + 1]).then_inc(unit_act, 1)
                elif w < U_G:
                    for t in range(TB):
                        unit_block(act, layer, t, T_WIN + w, last)
                        act.activation(v[:, t, cols(w - U_V)], ps[:, bank + t, :], ACT.Copy,
                                       scale=rstd[:, t:t + 1]).then_inc(unit_act, 1)
                else:
                    for t in range(TB):
                        unit_block(act, layer, t, T_WIN + w, last)
                        act.activation(swish_g[:, t, cols(w - U_G)], ps[:, bank + t, :], ACT.Silu,
                                       scale=rstd[:, t:t + 1]).then_inc(unit_act, 1)
                if U_QK + 2 <= w < U_QK + 6:
                    qk_copy(layer, w - U_QK - 2)

            act.dma_start(pos_i[:, :], positions).then_inc(rope_in, 16)
            act.dma_start(inv_sb[:, :], inv_freq).then_inc(rope_in, 16)
            act.dma_start(x_in[:, :, :], x.rearrange("b (t p) d -> p (b t) d", p=P)).then_inc(x_landed, 16)
            act.dma_start(ident[:, :], identity).then_inc(consts, 16)
            act.dma_start(vec[:, :, :], vectors[:, 0:NVEC, :]).then_inc(vec_landed, 16)
            act.dma_start(means[:, :], mean_matrix).then_inc(consts, 16)
            act.dma_start(decay_sb[:, :, :], decay).then_inc(consts, 16)
            act.wait_ge(start_step, ROPE_STEPS)
            act.activation(sin_sb[:, :, :], turns[:, :, :], ACT.Sin).then_inc(trig, 1)
            act.activation(cos_sb[:, :, :], turns_c[:, :, :], ACT.Sin).then_inc(trig, 1)

            with act.Fori(0, DEPTH) as layer:
                act.wait_ge(h_ready, layer * 16 + 4)
                act.dma_start(gate_bias[:, :], b_gates[bass.ds(layer, 1), :, :].rearrange("a g d -> (a g d)")
                              .partition_broadcast(P)).then_inc(bias_landed, 16)
                norm_his(layer, N_FFN1, (0, 1))
                split_hi(0, layer)
                norm_his(layer, N_FFN1, (2, 3))
                split_hi(1, layer)
                squares(layer, N_FFN1)
                ffn(layer, FFN1, N_FFN1, 0, T_FFN1)
                norm_his(layer, N_MIX, range(4))
                squares(layer, N_MIX)
                for u in range(WIN_UNITS):
                    if u == 1:
                        act.wait_ge(rstd_ready, layer * 4 + N_MIX + 1)
                    if u:
                        win_unit(layer, u - 1)
                    if u == 19:
                        head_squares(layer, 0)
                    split_hi(WIN + 2 * u + 2, layer)
                    split_hi(WIN + 2 * u + 3, layer)
                win_unit(layer, WIN_UNITS - 1)
                head_his(layer, 0)
                for hd in range(HEADS):
                    if hd == 3:
                        for i in range(2):
                            act.wait_ge(normed, layer * 2 + i + 1)
                            for k in range(4 * i, 4 * i + 4):
                                a = act.activation(yT[:, k, :], yT[:, k, :], ACT.Silu, bias=vec[:, V_LNB, k:k + 1],
                                                   scale=vec[:, V_LNG, k:k + 1])
                            a.then_inc(ln_silu, 1)
                            act.wait_ge(ln_silu, layer * 2 + i + 1)
                            act.activation(uT_hi[:, 4 * i:4 * i + 4, :], yT[:, 4 * i:4 * i + 4, :], ACT.Copy
                                           ).then_inc(ln_hi, 1)
                    split_hi(RET + 2 * hd + 2, layer)
                    if hd == 2:
                        act.wait_ge(var_eps, layer + 1)
                        act.activation(acted[:, 0, :], acted[:, 0, :], ACT.Sqrt).then_inc(std_ready, 1)
                    if hd + 1 < HEADS:
                        head_squares(layer, hd + 1)
                    if hd == 1:
                        for i in range(2):
                            act.wait_ge(centred, layer * 2 + i + 1)
                            act.activation(centred_sq[:, 4 * i:4 * i + 4, :], yT[:, 4 * i:4 * i + 4, :], ACT.Square
                                           ).then_inc(squared, 1)
                    split_hi(RET + 2 * hd + 3, layer)
                    if hd + 1 < HEADS:
                        head_his(layer, hd + 1)
                split_hi(CONVO + 2, layer)
                split_hi(CONVO + 3, layer)
                act.wait_ge(convT_lo, layer * 2 + 2)
                act.dma_start(p_in[:, :, :], p[bass.ds(layer, 1), :, :, :].rearrange("a b (t p) d -> p (a b t) d", p=P)
                              ).then_inc(p_landed, 16)
                act.wait_ge(score_done, layer * HEADS + HEADS)
                act.dma_start(gain_e[:, :], ple_gain[bass.ds(layer, 1), :].rearrange("a d -> (a d)")
                              .partition_broadcast(P)).then_inc(gain_landed, 16)
                act.dma_start(gain_f[:, :], final_gain.partition_broadcast(P)).then_inc(gain_landed, 16)
                split_hi(OUT, layer)
                m_his(layer, (0, 1))
                split_hi(OUT + 1, layer)
                split_hi(OUT + 2, layer)
                m_his(layer, (2, 3))
                split_hi(OUT + 3, layer)
                act.wait_ge(p_T, layer + 1)
                act.activation(hT_hi[:, 0:2, :], ps[:, T0, :].rearrange("p (k t) -> p k t", k=2), ACT.Copy
                               ).then_inc(p_hi, 1)
                split_hi(PLEP, layer)
                split_hi(FFN2, layer)
                norm_his(layer, N_FFN2, (0, 1))
                split_hi(FFN2 + 1, layer)
                norm_his(layer, N_FFN2, (2, 3))
                for i in range(4):
                    n, t = half_of(i)
                    last_piece(act, layer, i, P_E, PLEP)
                    if i:
                        act.wait_ge(e_squared, layer * 4 + i)
                    act.activation(junk[:, :], ps[:, i, :], ACT.Square, scale=D ** -0.5, accum_out=ssq_e[:, t, n:n + 1]
                                   ).then_inc(e_squared, 1)
                    act.activation(e_buf[:, t, cols(n)], ps[:, i, :], ACT.Copy).then_inc(e_evac, 1)
                act.wait_ge(e_squared, layer * 4 + 4)
                squares(layer, N_FFN2)
                act.wait_ge(norm_g, layer * 16 + N_FFN2 * 4 + 4)
                act.dma_start(vec[:, :, :], vectors[:, bass.ds((layer + 1) * NVEC, NVEC), :]).then_inc(vec_landed, 16)
                act.dma_start(vec_ple[:, :], vectors[:, bass.ds(layer * NVEC + V_PLE, 1), :].rearrange("p a k -> p (a k)")
                              ).then_inc(ple_landed, 16)
                ffn(layer, FFN2, N_FFN2, 15, T_FFN2)
                norm_his(layer, N_PLE, range(4))
                split_hi(PG + 2, layer)
                split_hi(PG + 3, layer)
                squares(layer, N_PLE)
                act.wait_ge(rstd_ready, layer * 4 + N_PLE + 1)
                for n in range(2):
                    for t in range(TB):
                        unit_block(act, layer, t, T_PG + n, PG + 2 * n + 1)
                        act.activation(gate_b[:, t, cols(n)], ps[:, (4, 0)[n] + t, :], ACT.Sigmoid,
                                       scale=rstd[:, t:t + 1]).then_inc(pg_act, 1)
            act.wait_ge(h_ready, DEPTH * 16 + 4)
            squares(DEPTH, N_FFN1)

        @block.vector
        def _(dve):
            def split_lo(c, layer, j=0):
                s = slot(c)
                dve.wait_ge(hi_done[s], nth(c, layer, j) + 1)
                dve.tensor_tensor(w_lo[:, s, :], raw[:, s, :], w_hi[:, s, :].bitcast(F32), ALU.subtract
                                  ).then_inc(lo_done[s], 1)

            def gains(layer, q, pieces):
                g = vec_ple if q == N_PLE else vec[:, (V_FFN1, V_MIX, V_FFN2)[q], :]
                for i in pieces:
                    n, t = half_of(i)
                    dve.wait_ge(norm_T, layer * 16 + q * 4 + i + 1)
                    if i >= 2:
                        dve.wait_ge(norm_lo, layer * 16 + q * 4 + i - 1)
                    dve.tensor_tensor(scaled[:, i % 2, :].rearrange("p (k t) -> p k t", k=4),
                                      ps[:, T0 + i % 2, :].rearrange("p (k t) -> p k t", k=4),
                                      g[:, 4 * n:4 * n + 4].unsqueeze(2).to_broadcast([P, 4, P]), ALU.mult
                                      ).then_inc(norm_g, 1)

            def norm_los(layer, q, pieces):
                for i in pieces:
                    n, t = half_of(i)
                    dve.wait_ge(norm_hi, layer * 16 + q * 4 + i + 1)
                    dve.tensor_tensor(uT_lo[:, 4 * n:4 * n + 4, toks(t)],
                                      scaled[:, i % 2, :].rearrange("p (k t) -> p k t", k=4),
                                      uT_hi[:, 4 * n:4 * n + 4, toks(t)].bitcast(F32), ALU.subtract
                                      ).then_inc(norm_lo, 1)

            def gated_product(layer, n, bank, j=0):
                for t in range(TB):
                    dve.wait_ge(acted_ready, layer * 52 + 2 * (n + j) + t + 1)
                    dve.scalar_tensor_tensor(mid[:, t, :], ps[:, bank + t, 256:512], rstd[:, t:t + 1], acted[:, t, :],
                                             ALU.mult, ALU.mult).then_inc(mid_ready, 1)

            def ffn(layer, F, mids):
                def mid_lower(k):
                    dve.wait_ge(mid_hi, layer * 26 + mids + k + 1)
                    dve.tensor_tensor(hT_lo[:, 0:2, :], ps[:, T0, :].rearrange("p (k t) -> p k t", k=2),
                                      hT_hi[:, 0:2, :].bitcast(F32), ALU.subtract).then_inc(mid_lo, 1)

                split_lo(F + 2, layer)
                gated_product(layer, mids, 4)
                split_lo(F + 3, layer)

                def unit(j):
                    mid_lower(j)
                    split_lo(F + 4, layer, j)
                    split_lo(F + 5, layer, j)
                    gated_product(layer, mids + 1, 4, j)
                    split_lo(F + 6, layer, j)

                unit(0)
                if F:
                    dve.wait_ge(e_r, layer + 1)
                    dve.wait_ge(gain_landed, 32 * layer + 32)
                    for t in range(TB):
                        dve.scalar_tensor_tensor(e_buf[:, t, :], e_buf[:, t, :], r_e[:, t:t + 1], gain_e[:, :],
                                                 ALU.mult, ALU.mult).then_inc(e_normed, 1)
                with dve.Fori(1, FFN_UNITS - 1) as j:
                    unit(j)
                mid_lower(FFN_UNITS - 1)
                split_lo(F + FFN_CHUNKS + 1, layer)

            def ffn_residual(layer, F, i):
                n, t = half_of(i)
                last_piece(dve, layer, i, P_FFN2 if F else P_FFN1, F + FFN_CHUNKS - 1)
                dve.scalar_tensor_tensor(h[:, t, cols(n)], ps[:, i, :], 0.5, h[:, t, cols(n)], ALU.mult, ALU.add
                                         ).then_inc(h_ready, 1)

            def after_ffn(layer, F, q):
                ffn_residual(layer, F, 0)
                ffn_residual(layer, F, 1)
                gains(layer, q, (0,))
                ffn_residual(layer, F, 2)
                gains(layer, q, (1,))
                norm_los(layer, q, (0,))
                ffn_residual(layer, F, 3)
                norm_los(layer, q, (1,))
                gains(layer, q, (2,))
                gains(layer, q, (3,))
                norm_los(layer, q, (2, 3))

            def conv_taps(layer):
                dve.wait_ge(mid_hi, layer * 26 + 15)
                for m in range(CONV_K * KT):
                    tap, k = m // KT, m % KT
                    src = gluT[:, k, tap:tap + SEQ]
                    weight = vec[:, V_TAPS + tap, k:k + 1]
                    if tap == 0:
                        op = dve.tensor_scalar(yT[:, k, :], src, weight, vec[:, V_CONVB, k:k + 1], ALU.mult, ALU.add)
                    else:
                        dve.wait_ge(conv_step, layer * CONV_K * KT + m - KT + 1)
                        op = dve.scalar_tensor_tensor(yT[:, k, :], src, weight, yT[:, k, :], ALU.mult, ALU.add)
                    op.then_inc(conv_step, 1)
                    yield

            def win_unit(layer, w):
                bank, last = w % 3 * 2, WIN + 2 * w + 1
                if w < U_GATE:
                    if w:
                        dve.wait_ge(mid_T, layer * 26 + 11 + w)
                    gated_product(layer, 11 + w, bank)
                elif w < U_QK:
                    g = w - U_GATE
                    dest = gate_a if g < 2 else gate_b
                    if g == 0:
                        dve.wait_ge(bias_landed, 16 * layer + 16)
                    for t in range(TB):
                        unit_block(dve, layer, t, T_WIN + w, last)
                        dve.scalar_tensor_tensor(dest[:, t, cols(g % 2)], ps[:, bank + t, :], rstd[:, t:t + 1],
                                                 gate_bias[:, cols(g)], ALU.mult, ALU.add).then_inc(gate_pre, 1)

            def decay_scores(layer, hd):
                dve.wait_ge(score_done, layer * HEADS + hd + 1)
                dve.tensor_tensor(scores[:, 0:SEQ], ps[:, T0, 0:SEQ], decay_sb[:, hd, :], ALU.mult)
                dve.tensor_tensor(scores[:, SEQ:3 * P], ps[:, T0, SEQ:3 * P], decay_sb[:, hd, 0:P], ALU.mult
                                  ).then_inc(decayed, 1)

            def head_outputs(layer, hd):
                dve.wait_ge(head_r, layer * HEADS + hd + 1)
                dve.wait_ge(unit_act, layer * 24 + 2 * (U_G - U_QK + hd) + 2)
                for t in range(TB):
                    dve.scalar_tensor_tensor(scaled[:, t, :], ps[:, 4 + t, :], r_head[:, t:t + 1],
                                             swish_g[:, t, hd * DV:(hd + 1) * DV], ALU.mult, ALU.mult
                                             ).then_inc(head_ready, 1)

            def head_los(layer, hd):
                for t in range(TB):
                    dve.wait_ge(head_hi, layer * 8 + 2 * hd + t + 1)
                    dve.tensor_tensor(hT_lo[:, :, toks(t)], ps[:, T1 - t, :].rearrange("p (k t) -> p k t", k=4),
                                      hT_hi[:, :, toks(t)].bitcast(F32), ALU.subtract).then_inc(head_lo, 1)

            def m_los(layer, pieces):
                for i in pieces:
                    n, t = half_of(i)
                    dve.wait_ge(m_hi, layer * 4 + i + 1)
                    dve.tensor_tensor(mT_lo[:, 4 * n:4 * n + 4, toks(t)],
                                      ps[:, T0 + i % 2, :].rearrange("p (k t) -> p k t", k=4),
                                      mT_hi[:, 4 * n:4 * n + 4, toks(t)].bitcast(F32), ALU.subtract
                                      ).then_inc(m_lo, 1)

            def conv_branch(layer, n):
                for t in range(TB):
                    unit_block(dve, layer, t, T_CONVO + n, CONVO + 2 * n + 1)
                    dve.tensor_tensor(gate_a[:, t, cols(n)], ps[:, (4, 0)[n] + t, :], gate_a[:, t, cols(n)], ALU.mult
                                      ).then_inc(conv_gated, 1)
                for t in range(TB):
                    dve.wait_ge(conv_gated, layer * 4 + 2 * n + t + 1)
                    dve.tensor_tensor(gate_a[:, t, cols(n)], gate_a[:, t, cols(n)], gate_b[:, t, cols(n)], ALU.add
                                      ).then_inc(m_ready, 1)

            done = [0]

            def step(op):
                done[0] += 1
                op.then_inc(start_step, 1)
                dve.wait_ge(start_step, done[0])

            for s in range(SLOTS):
                dve.sem_inc(lo_done[s], 1)
            dve.wait_ge(rope_in, 32)
            step(dve.tensor_copy(pos_f[:, :], pos_i[:, :]))
            for t in range(TB):
                step(dve.tensor_scalar(angle[:, t, :], inv_sb[:, :], pos_f[:, t:t + 1], None, ALU.mult))
            step(dve.tensor_scalar(turns[:, :, :], angle[:, :, :], 1.0 / TWO_PI, MAGIC, ALU.mult, ALU.add))
            step(dve.tensor_scalar(turns_c[:, :, :], angle[:, :, :], 1.0 / TWO_PI, 0.25, ALU.mult, ALU.add))
            step(dve.tensor_scalar(turns[:, :, :], turns[:, :, :], -MAGIC, None, ALU.add))
            step(dve.tensor_scalar(turns_c[:, :, :], turns_c[:, :, :], MAGIC, -MAGIC, ALU.add, ALU.add))
            for buf, keep in ((turns, 0), (turns_c, 1)):
                src = angle[:, :, :]
                for n, c in enumerate((C1, C2, C3)):
                    acc = junk[:, keep * 256:keep * 256 + 256].rearrange("p (t f) -> p t f", t=TB)
                    step(dve.scalar_tensor_tensor(acc, buf[:, :, :], -c, src, ALU.mult, ALU.add))
                    src = acc
                step(dve.tensor_scalar(acc, acc, TWO_PI / 4 if keep else 0.0, PI_IN, ALU.add, ALU.min))
                step(dve.tensor_scalar(buf[:, :, :], acc, -PI_IN, None, ALU.max))
            assert done[0] == ROPE_STEPS, done[0]
            dve.wait_ge(x_landed, 16)
            for i in range(4):
                n, t = half_of(i)
                dve.tensor_copy(h[:, t, cols(n)], x_in[:, t, cols(n)]).then_inc(h_ready, 1)

            with dve.Fori(0, DEPTH) as layer:
                dve.wait_ge(vec_landed, 16 * layer + 16)
                gains(layer, N_FFN1, (0, 1))
                norm_los(layer, N_FFN1, (0, 1))
                split_lo(0, layer)
                gains(layer, N_FFN1, (2, 3))
                norm_los(layer, N_FFN1, (2, 3))
                split_lo(1, layer)
                ffn(layer, FFN1, 0)
                after_ffn(layer, FFN1, N_MIX)
                taps = None
                for u in range(WIN_UNITS):
                    if u:
                        win_unit(layer, u - 1)
                    if u == 18:
                        decay_scores(layer, 0)
                    if u == 6:
                        taps = conv_taps(layer)
                    for c in range(2):
                        split_lo(WIN + 2 * u + 2 + c, layer)
                        if taps:
                            for _ in range(CONV_STEPS):
                                next(taps, None)
                head_outputs(layer, 0)
                head_los(layer, 0)
                for hd in range(HEADS):
                    if hd + 1 < HEADS:
                        decay_scores(layer, hd + 1)
                    if hd == 0:
                        for _ in taps:
                            pass
                    if hd == 3:
                        dve.wait_ge(ln_hi, layer * 2 + 1)
                        dve.tensor_tensor(uT_lo[:, 0:4, :], yT[:, 0:4, :], uT_hi[:, 0:4, :].bitcast(F32), ALU.subtract
                                          ).then_inc(convT_lo, 1)
                        dve.wait_ge(ln_hi, layer * 2 + 2)
                        dve.tensor_tensor(uT_lo[:, 4:8, :], yT[:, 4:8, :], uT_hi[:, 4:8, :].bitcast(F32), ALU.subtract
                                          ).then_inc(convT_lo, 1)
                    split_lo(RET + 2 * hd + 2, layer)
                    if hd == 1:
                        dve.wait_ge(mean_done, layer * 2 + 1)
                        for i in range(2):
                            part = yT[:, 4 * i:4 * i + 4, :]
                            dve.tensor_tensor(part, part, ps[:, T1, 0:SEQ].unsqueeze(1).to_broadcast([P, 4, SEQ]),
                                              ALU.subtract).then_inc(centred, 1)
                    if hd == 2:
                        dve.wait_ge(mean_done, layer * 2 + 2)
                        dve.tensor_scalar(acted[:, 0, :], ps[:, T1, 0:SEQ], EPS, None, ALU.add).then_inc(var_eps, 1)
                        dve.wait_ge(std_ready, layer + 1)
                        dve.reciprocal(acted[:, 0, :], acted[:, 0, :]).then_inc(ln_rstd, 1)
                        dve.wait_ge(ln_rstd, layer + 1)
                        for i in range(2):
                            part = yT[:, 4 * i:4 * i + 4, :]
                            dve.tensor_tensor(part, part, acted[:, 0, :].unsqueeze(1).to_broadcast([P, 4, SEQ]),
                                              ALU.mult).then_inc(normed, 1)
                    if hd + 1 < HEADS:
                        head_outputs(layer, hd + 1)
                    split_lo(RET + 2 * hd + 3, layer)
                    if hd + 1 < HEADS:
                        head_los(layer, hd + 1)
                for i in range(4):
                    n, t = half_of(i)
                    last_piece(dve, layer, i, P_RET, RET + 7)
                    dve.tensor_tensor(gate_b[:, t, cols(n)], ps[:, i, :], gate_b[:, t, cols(n)], ALU.mult
                                      ).then_inc(ret_gated, 1)
                split_lo(CONVO + 2, layer)
                split_lo(CONVO + 3, layer)
                conv_branch(layer, 0)
                split_lo(OUT, layer)
                m_los(layer, (0, 1))
                split_lo(OUT + 1, layer)
                conv_branch(layer, 1)
                split_lo(OUT + 2, layer)
                m_los(layer, (2, 3))
                split_lo(OUT + 3, layer)

                def out_residual(n):
                    for t in range(TB):
                        unit_block(dve, layer, t, T_OUT + n, OUT + 2 * n + 1)
                        dve.tensor_tensor(h[:, t, cols(n)], ps[:, (2, 4)[n] + t, :], h[:, t, cols(n)], ALU.add
                                          ).then_inc(h_ready, 1)

                out_residual(0)
                dve.wait_ge(p_hi, layer + 1)
                dve.tensor_tensor(hT_lo[:, 0:2, :], ps[:, T0, :].rearrange("p (k t) -> p k t", k=2),
                                  hT_hi[:, 0:2, :].bitcast(F32), ALU.subtract).then_inc(p_lo, 1)
                split_lo(PLEP, layer)
                split_lo(FFN2, layer)
                out_residual(1)
                gains(layer, N_FFN2, (0, 1))
                norm_los(layer, N_FFN2, (0, 1))
                split_lo(FFN2 + 1, layer)
                gains(layer, N_FFN2, (2, 3))
                norm_los(layer, N_FFN2, (2, 3))
                ffn(layer, FFN2, 15)
                dve.wait_ge(ple_landed, 16 * layer + 16)
                after_ffn(layer, FFN2, N_PLE)
                split_lo(PG + 2, layer)
                split_lo(PG + 3, layer)
                dve.wait_ge(e_normed, layer * TB + TB)
                for n in range(2):
                    for t in range(TB):
                        dve.wait_ge(pg_act, layer * 4 + 2 * n + t + 1)
                        dve.tensor_tensor(gate_b[:, t, cols(n)], gate_b[:, t, cols(n)], e_buf[:, t, cols(n)], ALU.mult
                                          ).then_inc(pg_prod, 1)
                    for t in range(TB):
                        dve.wait_ge(pg_prod, layer * 4 + 2 * n + t + 1)
                        dve.tensor_tensor(h[:, t, cols(n)], h[:, t, cols(n)], gate_b[:, t, cols(n)], ALU.add
                                          ).then_inc(h_ready, 1)
            dve.wait_ge(rstd_ready, DEPTH * 4 + 1)
            for t in range(TB):
                dve.scalar_tensor_tensor(e_buf[:, t, :], h[:, t, :], rstd[:, t:t + 1], gain_f[:, :], ALU.mult, ALU.mult
                                         ).then_inc(out_ready, 1)

        @block.gpsimd
        def _(pool):
            def inverse_root(mean, with_eps, result, steps):
                pool.tensor_tensor(with_eps, mean, eps_tile, ALU.add).then_inc(pool_step, 1)
                pool.wait_ge(pool_step, steps + 1)
                return pool.tensor_tensor(result, with_eps, minus_half, ALU.pow)

            def norm_rstd(layer, q, steps):
                pool.wait_ge(ssq_ready, layer * 16 + q * 4 + 4)
                pool.tensor_tensor(ssq_sum, ssq[:, :, 0], ssq[:, :, 1], ALU.add).then_inc(pool_step, 1)
                pool.wait_ge(pool_step, steps + 1)
                inverse_root(ssq_sum, ms, rstd, steps + 1).then_inc(rstd_ready, 1)

            pool.memset(minus_half, -0.5).then_inc(preset, 1)
            pool.memset(eps_tile, EPS).then_inc(preset, 1)
            pool.memset(gluT[:, :, 0:PAD], 0.0).then_inc(preset, 1)
            pool.wait_ge(preset, 3)
            pool.wait_ge(trig, 2)
            with pool.Fori(0, DEPTH) as layer:
                steps = layer * POOL_STEPS
                norm_rstd(layer, N_FFN1, steps)
                norm_rstd(layer, N_MIX, steps + 2)
                pool.wait_ge(gate_pre, layer * 8 + 8)
                for w in range(4):
                    pool.wait_ge(unit_act, layer * 24 + 2 * w + 2)
                    if w:
                        pool.wait_ge(qk_T, layer * 8 + 2 * w)
                    z = qk_in[:, w % 2]
                    t1, t2 = z[:, :, :, 0, :], z[:, :, :, 1, :]
                    cos = cos_sb[:, :, :].unsqueeze(2).to_broadcast([P, TB, 2, HALF])
                    sin = sin_sb[:, :, :].unsqueeze(2).to_broadcast([P, TB, 2, HALF])
                    pa, pb = prod_a[:, :, :, :], prod_b[:, :, :, :]
                    last = layer * 20 + 5 * w
                    pool.tensor_tensor(pa, t1, cos, ALU.mult).then_inc(rope_step, 1)
                    pool.tensor_tensor(pb, t2, sin, ALU.mult).then_inc(rope_step, 1)
                    pool.wait_ge(rope_step, last + 2)
                    pool.tensor_tensor(roped[:, :, :, 0, :], pa, pb, ALU.subtract).then_inc(rope_step, 1)
                    pool.wait_ge(rope_step, last + 3)
                    pool.tensor_tensor(pa, t2, cos, ALU.mult).then_inc(rope_step, 1)
                    pool.tensor_tensor(pb, t1, sin, ALU.mult).then_inc(rope_step, 1)
                    pool.wait_ge(rope_step, last + 5)
                    pool.tensor_tensor(roped[:, :, :, 1, :], pa, pb, ALU.add).then_inc(roped_ready, 1)
                for hd in range(HEADS):
                    pool.wait_ge(head_ssq, layer * 8 + 2 * hd + 2)
                    inverse_root(ssq_head, ms_head, r_head, steps + 4 + hd).then_inc(head_r, 1)
                pool.wait_ge(e_squared, layer * 4 + 4)
                pool.tensor_tensor(ssq_e_sum, ssq_e[:, :, 0], ssq_e[:, :, 1], ALU.add).then_inc(pool_step, 1)
                pool.wait_ge(pool_step, steps + 9)
                inverse_root(ssq_e_sum, ms_e, r_e, steps + 9).then_inc(e_r, 1)
                norm_rstd(layer, N_FFN2, steps + 10)
                norm_rstd(layer, N_PLE, steps + 12)
            norm_rstd(DEPTH, N_FFN1, DEPTH * POOL_STEPS)


def columns_chunks(w):
    return w.reshape(2, 4, P, COLS).transpose(0, 2, 1, 3).reshape(2, P, CHUNK)


def rows_chunks(w):
    return w.reshape(-1, 2, P, D).transpose(0, 2, 1, 3).reshape(-1, P, CHUNK)


def layer_chunks(i, w):
    def ffn(gate, up, down):
        down = rows_chunks(down)
        parts = []
        for k in range(FFN_UNITS):
            c = slice(256 * k, 256 * (k + 1))
            parts.append(columns_chunks(np.concatenate([gate[:, c], up[:, c]], axis=1)))
            if k:
                parts.append(down[k - 1:k])
        return parts + [down[-1:]]

    def units(m):
        return [columns_chunks(m[:, COLS * n:COLS * (n + 1)]) for n in range(m.shape[1] // COLS)]

    w_in = w["w_in"][i]
    conv_a, conv_b, q, k, v, g, gate_a, gate_b = np.split(w_in, np.cumsum([D, D, D, D, 2 * D, 2 * D, D]), axis=1)
    parts = ffn(w["ffn1_w_gate"][i], w["ffn1_w_up"][i], w["ffn1_w_down"][i])
    for n in range(4):
        c = slice(256 * n, 256 * (n + 1))
        parts.append(columns_chunks(np.concatenate([conv_b[:, c], conv_a[:, c]], axis=1)))
    for m in (gate_a, gate_b, q, k, v, g):
        parts += units(m)
    parts.append(rows_chunks(w["w_ret_o"][i]))
    parts += units(w["w_conv_o"][i]) + units(w["w_out"][i])
    parts.append(rows_chunks(w["w_ple_proj"][i]))
    parts += ffn(w["ffn2_w_gate"][i], w["ffn2_w_up"][i], w["ffn2_w_down"][i])
    parts += units(w["w_ple_gate"][i])
    return parts


def shape_constants():
    f = np.float32
    log_g = np.log1p(-np.exp2(f(-5.0) - np.arange(HEADS, dtype=f))).astype(f)
    rel = (np.arange(SEQ, dtype=f)[None, :] - np.arange(P, dtype=f)[:, None])
    decay = np.where(rel >= 0, np.exp(log_g[:, None, None] * np.maximum(rel, f(0)), dtype=f), f(0))
    decay = (decay * f(DK ** -0.5)).astype(f).transpose(1, 0, 2)
    inv = np.power(f(ROPE_BASE), -np.arange(HALF, dtype=f) / f(HALF)).astype(f)
    return {
        "decay": np.ascontiguousarray(decay),
        "inv_freq": np.ascontiguousarray(np.broadcast_to(inv, (P, HALF))),
        "identity": np.eye(P, dtype=f),
        "mean_matrix": np.full((P, P), 1.0 / D, dtype=f),
    }


def kernel(**inputs):
    import concourse.bacc as bacc
    from concourse.bass_utils import run_bass_kernel_spmd

    w = {name: np.asarray(a) for name, a in inputs.items()}
    parts = [c for i in range(DEPTH) for c in layer_chunks(i, w)]
    names = ["ffn1_norm", "mix_norm", "ffn2_norm", "ple_norm", "conv_b", "conv_ln_g", "conv_ln_b"]
    vectors = np.concatenate([np.stack([w[n] for n in names], axis=1), w["conv_w"]], axis=1)
    vectors = np.concatenate([vectors, vectors[:1]], axis=0)
    arrays = {
        "stream": np.concatenate(parts, axis=0),
        "x": w["x"], "p": w["p"], "positions": w["positions"].reshape(TB, P).T,
        "vectors": np.ascontiguousarray(vectors.reshape(-1, KT, P).transpose(2, 0, 1)),
        "b_gates": w["b_gates"], "ple_gain": w["ple_proj_norm"], "final_gain": w["final_norm"],
        **shape_constants(),
    }
    nc = bacc.Bacc("TRN2", target_bir_lowering=False, num_devices=1)
    arrays = {f"in_{n}": np.ascontiguousarray(a) for n, a in arrays.items()}
    args = [nc.dram_tensor(n, a.shape, mybir.dt.from_np(a.dtype), kind="ExternalInput").ap() for n, a in arrays.items()]
    out = nc.dram_tensor("out", (1, SEQ, D), F32, kind="ExternalOutput").ap()
    build_kernel(nc, *args, out)
    return run_bass_kernel_spmd(nc, [arrays], core_ids=[0]).results[0]["out"]
```

```python
from contextlib import ExitStack

import numpy as np

import concourse.bass as bass
from concourse import mybir

ALU = mybir.AluOpType
ACT = mybir.ActivationFunctionType
F32 = mybir.dt.float32
F32R = mybir.dt.float32r
I32 = mybir.dt.int32

P = 128
DEPTH = 2
D = 1024
SEQ = 256
TB = SEQ // P
KT = D // P
D_FF = ((8 * D // 3 + 127) // 128) * 128
PLE = 256
CONV_K = 31
HEADS = 4
DK = D // HEADS
DV = 2 * D // HEADS
EPS = 1e-6
ROPE_BASE = 10000.0
HALF = DK // 2
COLS = 512
CHUNK = 2048
SLOTS = 3
FFN_UNITS = D_FF // 256

FFN1 = 0
FFN_CHUNKS = 3 * FFN_UNITS
WIN = FFN1 + FFN_CHUNKS
WIN_UNITS = 20
RET = WIN + 2 * WIN_UNITS + 1
CONVO = RET + 2 * HEADS + 1
OUT = CONVO + 4
FFN2 = OUT + 5
PLEP = FFN2 + 1
PG = FFN2 + FFN_CHUNKS
LAYER = PG + 4
EMPTY = (RET - 1, CONVO - 1)
CHUNKS = LAYER - len(EMPTY)
assert LAYER % SLOTS == 0

U_CONV, U_GATE, U_QK, U_V, U_G = 0, 4, 8, 12, 16

V_FFN1, V_MIX, V_FFN2, V_PLE, V_CONVB, V_LNG, V_LNB, V_TAPS = 0, 1, 2, 3, 4, 5, 6, 7
NVEC = 7 + CONV_K

N_FFN1, N_MIX, N_FFN2, N_PLE = range(4)

MAGIC = 12582912.0
TWO_PI = 6.283185307179586
C1 = 6.28125
C2 = float(np.float32(TWO_PI - C1) - np.float32(np.float32(TWO_PI - C1) % np.float32(2.0 ** -20)))
C3 = TWO_PI - C1 - C2

PI_IN = 3.1415925
ROPE_STEPS = 17
POOL_STEPS = 14
POOL_SPLITS = (44, 46, 48, 50, 62, 64, 66, 68, 70, 72)
CONV_UNIT = 5


def conv_steps(u):
    return 0 if u < CONV_UNIT else 8 if u < U_QK + 1 else 7 if u < U_QK + 6 else 10 if u < U_G + 1 else 9



def slot(c):
    return c % SLOTS


def nth(c, layer, j=0):
    empty = [e for e in EMPTY if slot(e) == slot(c)]
    return layer * (LAYER // SLOTS - len(empty)) + c // SLOTS - sum(e < c for e in empty) + j


def ahead(c):
    for _ in range(2):
        c += 2 if c + 1 in EMPTY else 1
    return c


def build_kernel(nc, stream, x, p, positions, vectors, b_gates, ple_gain, final_gain,
                 decay, inv_freq, identity, mean_matrix, out):
    ctx = ExitStack()
    with ctx:
        def sem(name):
            return ctx.enter_context(nc.semaphore(name))

        top = [-(-nc.sbuf_base // 32) * 32]

        def at(name, shape, dt=F32, offset=None):
            n = 4 * int(np.prod(shape[1:]))
            o = top[0] if offset is None else offset
            if offset is None:
                top[0] += n
            return nc.alloc_sbuf_tensor_at(name, shape, dt, offset=o), o

        raw, _ = at("raw", [P, SLOTS, CHUNK])
        w_hi, _ = at("w_hi", [P, SLOTS, CHUNK], F32R)
        w_lo, _ = at("w_lo", [P, SLOTS, CHUNK], F32R)
        h, _ = at("h", [P, TB, D])
        uT_hi, _ = at("uT_hi", [P, KT, SEQ], F32R)
        uT_lo, o_uT_lo = at("uT_lo", [P, KT, SEQ], F32R)
        centred_sq, _ = at("centred_sq", [P, KT, SEQ], offset=o_uT_lo)
        gate_a, _ = at("gate_a", [P, TB, D])
        gate_b, _ = at("gate_b", [P, TB, D])
        v, o_v = at("v", [P, TB, HEADS * DV])
        mT_hi, _ = at("mT_hi", [P, KT, SEQ], F32R, offset=o_v)
        mT_lo, _ = at("mT_lo", [P, KT, SEQ], F32R, offset=o_v + 8192)
        swish_g, o_sg = at("swish_g", [P, TB, HEADS * DV])
        gate_bias, _ = at("gate_bias", [P, 2 * D], offset=o_sg)
        roped, _ = at("roped", [P, TB, 2, 2, HALF], offset=o_sg)
        prod_a, _ = at("prod_a", [P, TB, 2, HALF], offset=o_sg + 4096)
        prod_b, _ = at("prod_b", [P, TB, 2, HALF], offset=o_sg + 6144)
        qk_in, _ = at("qk_in", [P, 2, TB, 2, 2, HALF], offset=o_sg + 8192)
        qT, o_qT = at("qT", [P, KT, SEQ])
        kT, o_kT = at("kT", [P, KT, SEQ])
        e_buf, _ = at("e_buf", [P, TB, D], offset=o_qT)
        gain_e, _ = at("gain_e", [P, D], offset=o_kT)
        gain_f, _ = at("gain_f", [P, D], offset=o_kT + 4096)
        PAD = CONV_K - 1
        gluT, o_gluT = at("gluT", [P, KT, PAD + SEQ])
        oT_hi, _ = at("oT_hi", [P, 4, SEQ], F32R, offset=o_gluT)
        oT_lo, _ = at("oT_lo", [P, 4, SEQ], F32R, offset=o_gluT + 4096)
        yT, o_yT = at("yT", [P, KT, SEQ])
        p_in, _ = at("p_in", [P, TB, PLE], offset=o_yT)
        hT_hi, _ = at("hT_hi", [P, 4, SEQ], F32R)
        hT_lo, _ = at("hT_lo", [P, 4, SEQ], F32R)
        scaled, _ = at("scaled", [P, 2, 4 * P])
        acted, _ = at("acted", [P, TB, 256])
        mid, _ = at("mid", [P, TB, 256])
        junk, _ = at("junk", [P, COLS])
        scores, _ = at("scores", [P, 3 * P])
        decay_sb, _ = at("decay_sb", [P, HEADS, SEQ])
        cos_sb, _ = at("cos_sb", [P, TB, HALF])
        sin_sb, _ = at("sin_sb", [P, TB, HALF])
        ident, _ = at("ident", [P, P])
        means, _ = at("means", [P, P])
        vec, _ = at("vec", [P, NVEC, KT])
        vec_ple, _ = at("vec_ple", [P, KT])
        small, _ = at("small", [P, 64])
        angle, _ = at("angle", [P, TB, HALF], offset=o_v)
        turns, _ = at("turns", [P, TB, HALF], offset=o_v + 1024)
        turns_c, _ = at("turns_c", [P, TB, HALF], offset=o_v + 2048)
        inv_sb, _ = at("inv_sb", [P, HALF], offset=o_v + 3072)
        pos_i, _ = at("pos_i", [P, TB], I32, offset=o_v + 4096)
        pos_f, _ = at("pos_f", [P, TB], offset=o_v + 4128)
        assert top[0] <= nc.sbuf_usable_end, top[0]

        ssq = small[:, 0:4].rearrange("p (t n) -> p t n", t=TB)
        ms = small[:, 4:6]
        rstd = small[:, 6:8]
        ssq_head = small[:, 8:10]
        ms_head = small[:, 10:12]
        r_head = small[:, 12:14]
        ssq_e = small[:, 14:18].rearrange("p (t n) -> p t n", t=TB)
        ms_e = small[:, 18:20]
        r_e = small[:, 20:22]
        minus_half = small[:, 22:24]
        eps_tile = small[:, 28:30]
        zero = small[:, 30:31]
        ssq_sum = small[:, 24:26]
        ssq_e_sum = small[:, 26:28]

        ps = ctx.enter_context(nc.psum_tensor("ps", [P, 8, COLS], F32))
        T0, T1 = 6, 7

        landed = [sem(f"landed{s}") for s in range(SLOTS)]
        hi_done = [sem(f"hi_done{s}") for s in range(SLOTS)]
        lo_done = [sem(f"lo_done{s}") for s in range(SLOTS)]
        used = [sem(f"used{s}") for s in range(SLOTS)]
        tb0_done = sem("tb0_done")
        piece_done = sem("piece_done")
        h_ready = sem("h_ready")
        norm_T = sem("norm_T")
        norm_g = sem("norm_g")
        norm_hi = sem("norm_hi")
        norm_lo = sem("norm_lo")
        ssq_ready = sem("ssq_ready")
        rstd_ready = sem("rstd_ready")
        acted_ready = sem("acted_ready")
        mid_ready = sem("mid_ready")
        mid_T = sem("mid_T")
        mid_hi = sem("mid_hi")
        mid_lo = sem("mid_lo")
        unit_act = sem("unit_act")
        gate_pre = sem("gate_pre")
        gate_act = sem("gate_act")
        roped_ready = sem("roped_ready")
        rope_step = sem("rope_step")
        qk_T = sem("qk_T")
        qk_evac = sem("qk_evac")
        conv_step = sem("conv_step")
        mean_done = sem("mean_done")
        centred = sem("centred")
        squared = sem("squared")
        var_eps = sem("var_eps")
        std_ready = sem("std_ready")
        ln_rstd = sem("ln_rstd")
        normed = sem("normed")
        ln_silu = sem("ln_silu")
        ln_hi = sem("ln_hi")
        convT_lo = sem("convT_lo")
        score_done = sem("score_done")
        decayed = sem("decayed")
        pv_done = sem("pv_done")
        head_ssq = sem("head_ssq")
        head_r = sem("head_r")
        head_ready = sem("head_ready")
        head_T = sem("head_T")
        head_hi = sem("head_hi")
        head_lo = sem("head_lo")
        ret_gated = sem("ret_gated")
        conv_gated = sem("conv_gated")
        m_ready = sem("m_ready")
        m_T = sem("m_T")
        m_hi = sem("m_hi")
        m_lo = sem("m_lo")
        p_T = sem("p_T")
        p_hi = sem("p_hi")
        p_lo = sem("p_lo")
        e_squared = sem("e_squared")
        e_evac = sem("e_evac")
        e_r = sem("e_r")
        e_normed = sem("e_normed")
        pg_act = sem("pg_act")
        pg_prod = sem("pg_prod")
        pool_step = sem("pool_step")
        consts = sem("consts")
        consts_late = sem("consts_late")
        rope_in = sem("rope_in")
        x_landed = sem("x_landed")
        vec_landed = sem("vec_landed")
        ple_landed = sem("ple_landed")
        bias_landed = sem("bias_landed")
        p_landed = sem("p_landed")
        gain_landed = sem("gain_landed")
        start_step = sem("start_step")
        trig = sem("trig")
        padded = sem("padded")
        preset = sem("preset")
        out_ready = sem("out_ready")
        stored = sem("stored")

        head_T_parts = ((hT_hi, hT_lo), (oT_hi, oT_lo))

        def half_of(i):
            return i // TB, i % TB

        def cols(n):
            return slice(n * COLS, (n + 1) * COLS)

        def toks(t):
            return slice(t * P, (t + 1) * P)

        block = ctx.enter_context(nc.Block())

        @block.sync
        def _(sp):
            def load(c, layer, j=0):
                sp.wait_ge(lo_done[slot(c)], nth(c, layer, j) + 1)
                number = layer * CHUNKS + SLOTS * j + c - sum(e < c for e in EMPTY)
                sp.dma_start(raw[:, slot(c), :], stream[bass.ds(number, 1), :, :].rearrange("a p n -> p (a n)")
                             ).then_inc(landed[slot(c)], 16)

            sp.dma_start(inv_sb[:, :], inv_freq).then_inc(rope_in, 16)
            sp.dma_start(ident[:, :], identity).then_inc(consts, 16)
            with sp.Fori(0, DEPTH) as layer:
                for first, last in ((0, EMPTY[0]), (EMPTY[0] + 1, EMPTY[1]), (EMPTY[1] + 1, LAYER)):
                    rounds, rest = divmod(last - first, SLOTS)
                    with sp.Fori(0, rounds) as j:
                        for c in range(first, first + SLOTS):
                            load(c, layer, j)
                    for c in range(last - rest, last):
                        load(c, layer)
            for t in range(TB):
                sp.wait_ge(out_ready, t + 1)
                sp.dma_start(out[0, toks(t), :], e_buf[:, t, :]).then_inc(stored, 16)
            sp.wait_ge(stored, 16 * TB)

        @block.tensor
        def _(pe):
            def product(bank, lhs_hi, lhs_lo, kts, t, c, first, last, col=None):
                s = slot(c)
                steps = []
                for i, kt in enumerate(kts):
                    rows = slice(i * COLS, (i + 1) * COLS) if col is None else slice(i * D + col, i * D + col + COLS)
                    for a, b in ((lhs_hi, w_hi), (lhs_hi, w_lo), (lhs_lo, w_hi)):
                        steps.append((a[:, kt, toks(t)], b[:, s, rows]))
                for n, (a, b) in enumerate(steps):
                    mm = pe.matmul(ps[:, bank, :], a, b, start=first and n == 0, stop=last and n == len(steps) - 1)
                return mm

            def half_unit(c, layer, banks, lhs_hi, lhs_lo, second, j=0, before=(), between=()):
                pe.wait_ge(lo_done[slot(c)], nth(c, layer, j) + 2)
                kts = range(4, 8) if second else range(4)
                for t in range(TB):
                    if before:
                        pe.wait_ge(before[0], before[1] + t)
                    mm = product(banks[t], lhs_hi, lhs_lo, kts, t, c, not second, second)
                    if t == 1:
                        mm.then_inc(used[slot(c)], 1)
                    elif second:
                        mm.then_inc(tb0_done, 1)
                    if t == 0:
                        for do in between:
                            do()

            def first_unit(c, layer, banks, lhs_hi, lhs_lo, ready, pieces, rest):
                half_unit(c, layer, banks, lhs_hi, lhs_lo, False, before=(ready, pieces + 1), between=(rest,))
                half_unit(c + 1, layer, banks, lhs_hi, lhs_lo, True, before=(ready, pieces + 3))

            def rows_chunk(c, layer, lhs, kts, first, last, j=0, after=None, before=None):
                pe.wait_ge(lo_done[slot(c)], nth(c, layer, j) + 2)
                for i in range(4):
                    n, t = half_of(i)
                    if before and i in before:
                        pe.wait_ge(*before[i])
                    mm = product(i, *lhs, kts, t, c, first, last, col=n * COLS)
                    if i == 3:
                        mm.then_inc(used[slot(c)], 1)
                    elif last:
                        mm.then_inc(piece_done, 1)
                    if after and i in after:
                        after[i]()

            def transpose4(bank, pieces):
                for n, a in enumerate(pieces):
                    mm = pe.transpose(ps[:, bank, n * P:(n + 1) * P], a, ident[:, :])
                return mm

            def norm_transposes(layer, q, pieces=range(4)):
                for i in pieces:
                    n, t = half_of(i)
                    pe.wait_ge(h_ready, layer * 16 + q * 4 + i + 1)
                    if i >= 2:
                        pe.wait_ge(norm_g, layer * 16 + q * 4 + i - 1)
                    transpose4(T0 + i % 2, [h[:, t, n * COLS + k * P:n * COLS + (k + 1) * P] for k in range(4)]
                               ).then_inc(norm_T, 1)

            def mid_transposes(layer, n):
                pe.wait_ge(mid_ready, layer * 52 + 2 * n + 2)
                transpose4(T0, [mid[:, t, k * P:(k + 1) * P] for k in range(2) for t in range(TB)]
                           ).then_inc(mid_T, 1)

            def ffn(layer, F, q, mids, next_q):
                hT = (hT_hi, hT_lo)

                def down(c, j, kts=range(2), first=False, last=False, unit=0, after=None):
                    pe.wait_ge(mid_lo, layer * 22 + (11 if F else 0) + unit + j + 1)
                    rows_chunk(c, layer, hT, kts, first, last, j=j, after=after)

                first_unit(F - 1 if F else F, layer, (4, 5) if F else (2, 3), uT_hi, uT_lo, norm_lo, layer * 16 + q * 4,
                           lambda: norm_transposes(layer, q, (2, 3)))
                if F:
                    rows_chunk(PLEP, layer, (hT_hi, hT_lo), range(2), True, True)
                    mid_transposes(layer, mids)
                half_unit(F + 2, layer, (4, 5), uT_hi, uT_lo, False)
                if not F:
                    mid_transposes(layer, mids)
                half_unit(F + 3, layer, (4, 5), uT_hi, uT_lo, True)
                if F:
                    pe.wait_ge(e_evac, layer * 4 + 4)
                down(F + 4, 0, first=True)
                mid_transposes(layer, mids + 1)
                with pe.Fori(1, FFN_UNITS - 2) as j:
                    half_unit(F + 2, layer, (4, 5), uT_hi, uT_lo, False, j=j)
                    half_unit(F + 3, layer, (4, 5), uT_hi, uT_lo, True, j=j)
                    down(F + 4, j)
                    mid_transposes(layer, mids + 1 + j)
                j = FFN_UNITS - 2
                half_unit(F + 2, layer, (4, 5), uT_hi, uT_lo, False, j=j)
                half_unit(F + 3, layer, (4, 5), uT_hi, uT_lo, True, j=j)
                down(F + 4, j, after={1: lambda: mid_transposes(layer, mids + 1 + j)})
                down(F + FFN_CHUNKS - 1, 0, kts=range(2, 4), last=True, unit=FFN_UNITS - 1,
                     after={2: lambda: norm_transposes(layer, next_q, (0,)),
                            3: lambda: norm_transposes(layer, next_q, (1,))})

            def head_scores(layer, hd):
                bank = 4 if hd else T0
                pe.wait_ge(qk_evac, layer * 8 + 8)
                for k in range(2):
                    pe.matmul(ps[:, bank, 0:SEQ], kT[:, 2 * hd + k, 0:P], qT[:, 2 * hd + k, :],
                              start=k == 0, stop=k == 1)
                for k in range(2):
                    mm = pe.matmul(ps[:, bank, SEQ:SEQ + P], kT[:, 2 * hd + k, P:SEQ], qT[:, 2 * hd + k, P:SEQ],
                                   start=k == 0, stop=k == 1)
                mm.then_inc(score_done, 1)

            def head_values(layer, hd):
                pe.wait_ge(decayed, layer * HEADS + hd + 1)
                cv = slice(hd * DV, (hd + 1) * DV)
                pe.matmul(ps[:, 4, :], scores[:, 0:P], v[:, 0, cv], start=True, stop=True).then_inc(pv_done, 1)
                pe.matmul(ps[:, 5, :], scores[:, P:SEQ], v[:, 0, cv], start=True, stop=False)
                pe.matmul(ps[:, 5, :], scores[:, SEQ:3 * P], v[:, 1, cv], start=False, stop=True).then_inc(pv_done, 1)

            def head_transposes(layer, hd):
                for t in range(TB):
                    pe.wait_ge(head_ready, layer * 8 + 2 * hd + t + 1)
                    transpose4(T1 - t, [scaled[:, t, k * P:(k + 1) * P] for k in range(4)]).then_inc(head_T, 1)

            def m_transposes(layer, pieces):
                for i in pieces:
                    n, t = half_of(i)
                    pe.wait_ge(m_ready, layer * 4 + i + 1)
                    if i >= 2:
                        pe.wait_ge(m_lo, layer * 4 + i - 1)
                    transpose4(T0 + i % 2, [gate_a[:, t, n * COLS + k * P:n * COLS + (k + 1) * P] for k in range(4)]
                               ).then_inc(m_T, 1)

            for s in range(SLOTS):
                pe.sem_inc(used[s], 1)
            pe.wait_ge(consts, 16)
            pe.wait_ge(x_landed, 16)
            pe.sem_inc(h_ready, 4)
            norm_transposes(0, N_FFN1, (0, 1))
            with pe.Fori(0, DEPTH) as layer:
                ffn(layer, FFN1, N_FFN1, 0, N_MIX)
                for u in range(WIN_UNITS):
                    banks = (u % 3 * 2, u % 3 * 2 + 1)
                    w = u - 3
                    if U_CONV <= w < U_GATE:
                        pe.wait_ge(mid_ready, layer * 52 + 22 + 2 * w + 2)
                    elif U_GATE <= w < U_QK:
                        pe.wait_ge(gate_pre, layer * 8 + 2 * (w - U_GATE) + 2)
                    elif U_QK <= w:
                        pe.wait_ge(unit_act, layer * 24 + 2 * (w - U_QK) + 2)
                    if u == 0:
                        first_unit(WIN, layer, banks, uT_hi, uT_lo, norm_lo, layer * 16 + N_MIX * 4,
                                   lambda: norm_transposes(layer, N_MIX, (2, 3)))
                    else:
                        half_unit(WIN + 2 * u, layer, banks, uT_hi, uT_lo, False)
                        half_unit(WIN + 2 * u + 1, layer, banks, uT_hi, uT_lo, True)
                    if U_CONV < u <= U_GATE:
                        if u - 1 > U_CONV:
                            pe.wait_ge(mid_hi, layer * 26 + 11 + u - 1)
                        mid_transposes(layer, 11 + u - 1)
                    if U_QK + 2 <= u < U_QK + 6:
                        w = u - 2 - U_QK
                        pe.wait_ge(roped_ready, layer * 4 + w + 1)
                        for t in range(TB):
                            if w:
                                pe.wait_ge(qk_evac, layer * 8 + 2 * (w - 1) + t + 1)
                            transpose4(T0 + t, [roped[:, t, k // 2, k % 2, :] for k in range(4)]).then_inc(qk_T, 1)
                    if u == 17:
                        head_scores(layer, 0)
                    if u == 18:
                        pe.wait_ge(unit_act, layer * 24 + 2 * (17 - U_QK) + 2)
                        head_values(layer, 0)
                    if u == 19:
                        head_transposes(layer, 0)
                        head_scores(layer, 1)
                pe.wait_ge(unit_act, layer * 24 + 22)
                for hd in range(HEADS):
                    if hd == 1:
                        pe.wait_ge(head_lo, layer * 8 + 2 * hd + 1)
                        pe.wait_ge(conv_step, (layer + 1) * CONV_K * KT)
                        pe.wait_ge(consts_late, 32)
                        for k in range(KT):
                            mm = pe.matmul(ps[:, T1, 0:SEQ], means[:, :], yT[:, k, :], start=k == 0, stop=k == KT - 1)
                        mm.then_inc(mean_done, 1)
                    if hd == 2:
                        pe.wait_ge(head_lo, layer * 8 + 2 * hd + 1)
                        pe.wait_ge(squared, layer * 2 + 2)
                        for k in range(KT):
                            mm = pe.matmul(ps[:, T1, 0:SEQ], means[:, :], centred_sq[:, k, :], start=k == 0, stop=k == KT - 1)
                        mm.then_inc(mean_done, 1)
                    lhs = head_T_parts[hd % 2]
                    more = hd + 1 < HEADS

                    def next_values():
                        head_values(layer, hd + 1)
                        if hd == 0:
                            pe.wait_ge(unit_act, layer * 24 + 24)

                    def next_transposes():
                        if hd == 1:
                            pe.wait_ge(centred, layer * 2 + 2)
                        if hd == 2:
                            pe.wait_ge(var_eps, layer + 1)
                        head_transposes(layer, hd + 1)
                        if hd + 2 < HEADS:
                            head_scores(layer, hd + 2)

                    rows_chunk(RET + 2 * hd, layer, lhs, range(2), hd == 0, False,
                               before={t: (head_lo, layer * 8 + 2 * hd + t + 1) for t in range(TB)},
                               after={1: next_values} if more else None)
                    rows_chunk(RET + 2 * hd + 1, layer, lhs, range(2, 4), False, not more,
                               after={1: next_transposes} if more else None)
                half_unit(CONVO, layer, (4, 5), uT_hi, uT_lo, False, before=(convT_lo, layer * 4 + 1))
                half_unit(CONVO + 1, layer, (4, 5), uT_hi, uT_lo, True, before=(convT_lo, layer * 4 + 3))
                pe.wait_ge(ret_gated, layer * 4 + 2)
                half_unit(CONVO + 2, layer, (0, 1), uT_hi, uT_lo, False)
                m_transposes(layer, (0, 1))
                half_unit(CONVO + 3, layer, (0, 1), uT_hi, uT_lo, True)
                pe.wait_ge(ret_gated, layer * 4 + 4)
                first_unit(OUT, layer, (2, 3), mT_hi, mT_lo, m_lo, layer * 4, lambda: m_transposes(layer, (2, 3)))
                pe.wait_ge(p_landed, layer * 16 + 16)
                transpose4(T0, [p_in[:, t, k * P:(k + 1) * P] for k in range(2) for t in range(TB)]).then_inc(p_T, 1)
                half_unit(OUT + 2, layer, (0, 1), mT_hi, mT_lo, False)
                pe.wait_ge(p_lo, layer + 1)
                norm_transposes(layer, N_FFN2, (0,))
                norm_transposes(layer, N_FFN2, (1,))
                half_unit(OUT + 3, layer, (0, 1), mT_hi, mT_lo, True)
                ffn(layer, FFN2, N_FFN2, 15, N_PLE)
                first_unit(PG, layer, (4, 5), uT_hi, uT_lo, norm_lo, layer * 16 + N_PLE * 4,
                           lambda: norm_transposes(layer, N_PLE, (2, 3)))
                half_unit(PG + 2, layer, (0, 1), uT_hi, uT_lo, False)
                half_unit(PG + 3, layer, (0, 1), uT_hi, uT_lo, True,
                          between=(lambda: norm_transposes(layer + 1, N_FFN1, (0, 1)),))

        T_FFN1, T_WIN, T_CONVO, T_OUT, T_FFN2, T_PG, T_LAYER = 0, 11, 31, 33, 35, 46, 48
        P_FFN1, P_RET, P_E, P_FFN2, P_LAYER = 0, 3, 6, 9, 12

        def unit_block(eng, layer, t, first_index, last_chunk, j=0, k=0):
            if t == 0:
                eng.wait_ge(tb0_done, layer * T_LAYER + first_index + k + 1)
            else:
                eng.wait_ge(used[slot(last_chunk)], nth(last_chunk, layer, j) + 2)

        def last_piece(eng, layer, i, first_index, last_chunk):
            if i < 3:
                eng.wait_ge(piece_done, layer * P_LAYER + first_index + i + 1)
            else:
                eng.wait_ge(used[slot(last_chunk)], nth(last_chunk, layer) + 2)

        @block.scalar
        def _(act):
            def split_hi(c, layer, j=0):
                s = slot(c)
                act.wait_ge(landed[s], 16 * (nth(c, layer, j) + 1))
                act.wait_ge(used[s], nth(c, layer, j) + 1)
                act.activation(w_hi[:, s, :], raw[:, s, :], ACT.Copy).then_inc(hi_done[s], 1)

            def norm_his(layer, q, pieces):
                for i in pieces:
                    n, t = half_of(i)
                    act.wait_ge(norm_g, layer * 16 + q * 4 + i + 1)
                    act.activation(uT_hi[:, 4 * n:4 * n + 4, toks(t)],
                                   scaled[:, i % 2, :].rearrange("p (k t) -> p k t", k=4),
                                   ACT.Copy).then_inc(norm_hi, 1)

            def squares(layer, q, pieces=range(4)):
                for i in pieces:
                    n, t = half_of(i)
                    act.wait_ge(h_ready, layer * 16 + q * 4 + i + 1)
                    if i:
                        act.wait_ge(ssq_ready, layer * 16 + q * 4 + i)
                    act.activation(junk[:, :], h[:, t, cols(n)], ACT.Square, scale=D ** -0.5,
                                   accum_out=ssq[:, t, n:n + 1]).then_inc(ssq_ready, 1)

            def gated(layer, n, func, first_index, last_chunk, j=0, k=0):
                for t in range(TB):
                    unit_block(act, layer, t, first_index, last_chunk, j, k)
                    act.activation(acted[:, t, :], ps[:, n + t, 0:256], func, scale=rstd[:, t:t + 1]
                                   ).then_inc(acted_ready, 1)

            def ffn(layer, F, q, mids, first_index):
                def mid_upper(k, to=0):
                    act.wait_ge(mid_T, layer * 26 + mids + k + 1)
                    act.activation(hT_hi[:, to:to + 2, :], ps[:, T0, :].rearrange("p (k t) -> p k t", k=2),
                                   ACT.Copy).then_inc(mid_hi, 1)

                act.wait_ge(rstd_ready, layer * 4 + q + 1)
                gated(layer, 4 if F else 2, ACT.Silu, first_index, F if F else F + 1)
                split_hi(F + 3, layer)
                if F:
                    for i in range(4):
                        n, t = half_of(i)
                        last_piece(act, layer, i, P_E, PLEP)
                        act.activation(e_buf[:, t, cols(n)], ps[:, i, :], ACT.Copy).then_inc(e_evac, 1)

                def unit(j, first=False):
                    mid_upper(j)
                    if F and first:
                        for i in range(4):
                            n, t = half_of(i)
                            act.wait_ge(e_evac, layer * 4 + i + 1)
                            if i:
                                act.wait_ge(e_squared, layer * 4 + i)
                            else:
                                act.wait_ge(ssq_ready, layer * 16 + N_FFN2 * 4 + 4)
                            act.activation(junk[:, :], e_buf[:, t, cols(n)], ACT.Square, scale=D ** -0.5,
                                           accum_out=ssq_e[:, t, n:n + 1]).then_inc(e_squared, 1)
                        act.wait_ge(e_squared, layer * 4 + 4)
                    split_hi(F + 4, layer, j)
                    split_hi(F + 5, layer, j)
                    gated(layer, 4, ACT.Silu, first_index + 1, F + 3, j, j)
                    split_hi(F + 6, layer, j)

                unit(0, True)
                with act.Fori(1, FFN_UNITS - 1) as j:
                    unit(j)
                mid_upper(FFN_UNITS - 1, 2)
                act.preload_act_table(ACT.Sigmoid)
                split_hi(F + FFN_CHUNKS + 1, layer)

            def head_squares(layer, hd):
                for t in range(TB):
                    act.wait_ge(pv_done, layer * 8 + 2 * hd + t + 1)
                    if t:
                        act.wait_ge(head_ssq, layer * 8 + 2 * hd + t)
                    act.activation(junk[:, :], ps[:, 4 + t, :], ACT.Square, scale=DV ** -0.5,
                                   accum_out=ssq_head[:, t:t + 1]).then_inc(head_ssq, 1)

            def head_his(layer, hd):
                if hd == 1:
                    act.wait_ge(conv_step, (layer + 1) * CONV_K * KT)
                for t in range(TB):
                    act.wait_ge(head_T, layer * 8 + 2 * hd + t + 1)
                    act.activation(head_T_parts[hd % 2][0][:, :, toks(t)], ps[:, T1 - t, :].rearrange("p (k t) -> p k t", k=4),
                                   ACT.Copy).then_inc(head_hi, 1)

            def m_his(layer, pieces):
                for i in pieces:
                    n, t = half_of(i)
                    act.wait_ge(m_T, layer * 4 + i + 1)
                    act.activation(mT_hi[:, 4 * n:4 * n + 4, toks(t)],
                                   ps[:, T0 + i % 2, :].rearrange("p (k t) -> p k t", k=4),
                                   ACT.Copy).then_inc(m_hi, 1)

            def glu_copy(layer, w):
                act.wait_ge(mid_T, layer * 26 + 11 + w + 1)
                act.activation(gluT[:, 2 * w:2 * w + 2, PAD:PAD + SEQ],
                               ps[:, T0, :].rearrange("p (k t) -> p k t", k=2), ACT.Copy).then_inc(mid_hi, 1)

            def qk_copy(layer, w):
                dest = qT if w < 2 else kT
                for t in range(TB):
                    act.wait_ge(qk_T, layer * 8 + 2 * w + t + 1)
                    act.activation(dest[:, 4 * (w % 2):4 * (w % 2) + 4, toks(t)],
                                   ps[:, T0 + t, :].rearrange("p (k t) -> p k t", k=4), ACT.Copy).then_inc(qk_evac, 1)

            def win_unit(layer, w):
                bank, last = w % 3 * 2, WIN + 2 * w + 1
                if w < U_GATE:
                    if w:
                        act.wait_ge(mid_ready, layer * 52 + 22 + 2 * w)
                    gated(layer, bank, ACT.Sigmoid, T_WIN + w, last)
                    if w:
                        glu_copy(layer, w - 1)
                elif w < U_QK:
                    g = w - U_GATE
                    dest = gate_a if g < 2 else gate_b
                    if g == 0:
                        glu_copy(layer, U_GATE - 1)
                    act.wait_ge(gate_pre, layer * 8 + 2 * g + 2)
                    act.activation(dest[:, :, cols(g % 2)], dest[:, :, cols(g % 2)], ACT.Sigmoid).then_inc(gate_act, 1)
                elif w < U_V:
                    r = w - U_QK
                    if r >= 2:
                        act.wait_ge(roped_ready, layer * 4 + r - 1)
                    for t in range(TB):
                        unit_block(act, layer, t, T_WIN + w, last)
                        act.activation(qk_in[:, r % 2, t].rearrange("p h a c -> p (h a c)"), ps[:, bank + t, :],
                                       ACT.Copy, scale=rstd[:, t:t + 1]).then_inc(unit_act, 1)
                elif w < U_G:
                    for t in range(TB):
                        unit_block(act, layer, t, T_WIN + w, last)
                        act.activation(v[:, t, cols(w - U_V)], ps[:, bank + t, :], ACT.Copy,
                                       scale=rstd[:, t:t + 1]).then_inc(unit_act, 1)
                else:
                    for t in range(TB):
                        unit_block(act, layer, t, T_WIN + w, last)
                        act.activation(swish_g[:, t, cols(w - U_G)], ps[:, bank + t, :], ACT.Silu,
                                       scale=rstd[:, t:t + 1]).then_inc(unit_act, 1)
                if U_QK + 2 <= w < U_QK + 6:
                    qk_copy(layer, w - U_QK - 2)

            act.dma_start(pos_i[:, :], positions).then_inc(rope_in, 16)
            act.dma_start(vec[:, :, :], vectors[:, 0:NVEC, :]).then_inc(vec_landed, 16)
            act.dma_start(h[:, :, :], x.rearrange("b (t p) d -> p (b t) d", p=P)).then_inc(x_landed, 16)
            act.dma_start(means[:, :], mean_matrix).then_inc(consts_late, 16)
            act.dma_start(decay_sb[:, :, :], decay).then_inc(consts_late, 16)
            act.preload_act_table(ACT.Silu)
            split_hi(0, 0)
            norm_his(0, N_FFN1, (0, 1))
            split_hi(1, 0)
            squares(0, N_FFN1, range(4))
            act.wait_ge(start_step, ROPE_STEPS)
            act.activation(sin_sb[:, :, :], turns[:, :, :], ACT.Sin).then_inc(trig, 1)
            act.activation(cos_sb[:, :, :], turns_c[:, :, :], ACT.Sin).then_inc(trig, 1)
            with act.Fori(0, DEPTH) as layer:
                act.wait_ge(h_ready, layer * 16 + 4)
                act.dma_start(gate_bias[:, :], b_gates[bass.ds(layer, 1), :, :].rearrange("a g d -> (a g d)")
                              .partition_broadcast(P)).then_inc(bias_landed, 16)
                split_hi(FFN1 + 2, layer)
                norm_his(layer, N_FFN1, (2, 3))
                ffn(layer, FFN1, N_FFN1, 0, T_FFN1)
                norm_his(layer, N_MIX, (0, 1))
                split_hi(WIN + 2, layer)
                norm_his(layer, N_MIX, (2, 3))
                squares(layer, N_MIX)
                for u in range(WIN_UNITS):
                    if u == 1:
                        act.wait_ge(rstd_ready, layer * 4 + N_MIX + 1)
                    if u and not U_GATE < u <= U_QK:
                        win_unit(layer, u - 1)
                    if u == U_QK + 2:
                        act.preload_act_table(ACT.Silu)
                    if u == 19:
                        head_squares(layer, 0)
                    if u:
                        split_hi(ahead(WIN + 2 * u), layer)
                    if U_GATE < u <= U_QK:
                        win_unit(layer, u - 1)
                    split_hi(ahead(WIN + 2 * u + 1), layer)
                head_his(layer, 0)
                win_unit(layer, WIN_UNITS - 1)
                for hd in range(HEADS):
                    if hd == 3:
                        for i in range(2):
                            act.wait_ge(normed, layer * 2 + i + 1)
                            for k in range(4 * i, 4 * i + 4):
                                a = act.activation(yT[:, k, :], yT[:, k, :], ACT.Silu, bias=vec[:, V_LNB, k:k + 1],
                                                   scale=vec[:, V_LNG, k:k + 1])
                            a.then_inc(ln_silu, 1)
                            act.wait_ge(ln_silu, layer * 2 + i + 1)
                            act.activation(uT_hi[:, 4 * i:4 * i + 4, :], yT[:, 4 * i:4 * i + 4, :], ACT.Copy
                                           ).then_inc(ln_hi, 1)
                    split_hi(ahead(RET + 2 * hd), layer)
                    if hd == 2:
                        act.wait_ge(var_eps, layer + 1)
                        act.activation(acted[:, 0, :], acted[:, 0, :], ACT.Sqrt).then_inc(std_ready, 1)
                    if hd + 1 < HEADS:
                        head_squares(layer, hd + 1)
                    if hd == 1:
                        for i in range(2):
                            act.wait_ge(centred, layer * 2 + i + 1)
                            act.activation(centred_sq[:, 4 * i:4 * i + 4, :], yT[:, 4 * i:4 * i + 4, :], ACT.Square
                                           ).then_inc(squared, 1)
                    split_hi(ahead(RET + 2 * hd + 1), layer)
                    if hd + 1 < HEADS:
                        head_his(layer, hd + 1)
                split_hi(CONVO + 2, layer)
                split_hi(CONVO + 3, layer)
                act.wait_ge(convT_lo, layer * 4 + 4)
                act.dma_start(p_in[:, :, :], p[bass.ds(layer, 1), :, :, :].rearrange("a b (t p) d -> p (a b t) d", p=P)
                              ).then_inc(p_landed, 16)
                act.wait_ge(score_done, layer * HEADS + HEADS)
                act.dma_start(gain_e[:, :], ple_gain[bass.ds(layer, 1), :].rearrange("a d -> (a d)")
                              .partition_broadcast(P)).then_inc(gain_landed, 16)
                act.dma_start(gain_f[:, :], final_gain.partition_broadcast(P)).then_inc(gain_landed, 16)
                split_hi(OUT, layer)
                m_his(layer, (0, 1))
                split_hi(OUT + 1, layer)
                split_hi(OUT + 2, layer)
                m_his(layer, (2, 3))
                split_hi(OUT + 3, layer)
                act.wait_ge(p_T, layer + 1)
                act.activation(hT_hi[:, 0:2, :], ps[:, T0, :].rearrange("p (k t) -> p k t", k=2), ACT.Copy
                               ).then_inc(p_hi, 1)
                split_hi(FFN2 - 1, layer)
                norm_his(layer, N_FFN2, (0, 1))
                split_hi(FFN2, layer)
                split_hi(PLEP, layer)
                norm_his(layer, N_FFN2, (2, 3))
                squares(layer, N_FFN2)
                split_hi(FFN2 + 2, layer)
                act.wait_ge(norm_g, layer * 16 + N_FFN2 * 4 + 4)
                act.dma_start(vec[:, :, :], vectors[:, bass.ds((layer + 1) * NVEC, NVEC), :]).then_inc(vec_landed, 16)
                act.dma_start(vec_ple[:, :], vectors[:, bass.ds(layer * NVEC + V_PLE, 1), :].rearrange("p a k -> p (a k)")
                              ).then_inc(ple_landed, 16)
                ffn(layer, FFN2, N_FFN2, 15, T_FFN2)
                norm_his(layer, N_PLE, (0, 1))
                split_hi(PG + 2, layer)
                norm_his(layer, N_PLE, (2, 3))
                squares(layer, N_PLE)
                split_hi(PG + 3, layer)
                with act.If(DEPTH - 1 - layer):
                    split_hi(LAYER, layer)
                act.wait_ge(rstd_ready, layer * 4 + N_PLE + 1)
                for n in range(2):
                    if n:
                        squares(layer + 1, N_FFN1, (0, 1))
                        with act.If(DEPTH - 1 - layer):
                            split_hi(LAYER + 1, layer)
                            norm_his(layer + 1, N_FFN1, (0, 1))
                    for t in range(TB):
                        unit_block(act, layer, t, T_PG + n, PG + 2 * n + 1)
                        act.activation(gate_b[:, t, cols(n)], ps[:, (4, 0)[n] + t, :], ACT.Sigmoid,
                                       scale=rstd[:, t:t + 1]).then_inc(pg_act, 1)
                squares(layer + 1, N_FFN1, (2, 3))
                act.preload_act_table(ACT.Silu)

        @block.vector
        def _(dve):
            def split_lo(c, layer, j=0):
                s = slot(c)
                dve.wait_ge(hi_done[s], nth(c, layer, j) + 1)
                dve.tensor_tensor(w_lo[:, s, :], raw[:, s, :], w_hi[:, s, :].bitcast(F32), ALU.subtract
                                  ).then_inc(lo_done[s], 1)

            def gains(layer, q, pieces):
                g = vec_ple if q == N_PLE else vec[:, (V_FFN1, V_MIX, V_FFN2)[q], :]
                for i in pieces:
                    n, t = half_of(i)
                    dve.wait_ge(norm_T, layer * 16 + q * 4 + i + 1)
                    if i >= 2:
                        dve.wait_ge(norm_lo, layer * 16 + q * 4 + i - 1)
                    dve.tensor_tensor(scaled[:, i % 2, :].rearrange("p (k t) -> p k t", k=4),
                                      ps[:, T0 + i % 2, :].rearrange("p (k t) -> p k t", k=4),
                                      g[:, 4 * n:4 * n + 4].unsqueeze(2).to_broadcast([P, 4, P]), ALU.mult
                                      ).then_inc(norm_g, 1)

            def norm_los(layer, q, pieces):
                for i in pieces:
                    n, t = half_of(i)
                    dve.wait_ge(norm_hi, layer * 16 + q * 4 + i + 1)
                    dve.tensor_tensor(uT_lo[:, 4 * n:4 * n + 4, toks(t)],
                                      scaled[:, i % 2, :].rearrange("p (k t) -> p k t", k=4),
                                      uT_hi[:, 4 * n:4 * n + 4, toks(t)].bitcast(F32), ALU.subtract
                                      ).then_inc(norm_lo, 1)

            def gated_product(layer, n, bank, j=0):
                for t in range(TB):
                    dve.wait_ge(acted_ready, layer * 52 + 2 * (n + j) + t + 1)
                    dve.scalar_tensor_tensor(mid[:, t, :], ps[:, bank + t, 256:512], rstd[:, t:t + 1], acted[:, t, :],
                                             ALU.mult, ALU.mult).then_inc(mid_ready, 1)

            def ffn(layer, F, mids):
                def mid_lower(k, to=0):
                    dve.wait_ge(mid_hi, layer * 26 + mids + k + 1)
                    dve.tensor_tensor(hT_lo[:, to:to + 2, :], ps[:, T0, :].rearrange("p (k t) -> p k t", k=2),
                                      hT_hi[:, to:to + 2, :].bitcast(F32), ALU.subtract).then_inc(mid_lo, 1)

                split_lo(F + 2, layer)
                gated_product(layer, mids, 4 if F else 2)
                split_lo(F + 3, layer)

                def unit(j):
                    mid_lower(j)
                    split_lo(F + 4, layer, j)
                    split_lo(F + 5, layer, j)
                    gated_product(layer, mids + 1, 4, j)
                    split_lo(F + 6, layer, j)

                unit(0)
                if F:
                    dve.wait_ge(e_r, layer + 1)
                    dve.wait_ge(gain_landed, 32 * layer + 32)
                    for t in range(TB):
                        dve.scalar_tensor_tensor(e_buf[:, t, :], e_buf[:, t, :], r_e[:, t:t + 1], gain_e[:, :],
                                                 ALU.mult, ALU.mult).then_inc(e_normed, 1)
                with dve.Fori(1, FFN_UNITS - 1) as j:
                    unit(j)
                mid_lower(FFN_UNITS - 1, 2)

            def ffn_residual(layer, F, i):
                n, t = half_of(i)
                last_piece(dve, layer, i, P_FFN2 if F else P_FFN1, F + FFN_CHUNKS - 1)
                dve.scalar_tensor_tensor(h[:, t, cols(n)], ps[:, i, :], 0.5, h[:, t, cols(n)], ALU.mult, ALU.add
                                         ).then_inc(h_ready, 1)

            def after_ffn(layer, F, q):
                ffn_residual(layer, F, 0)
                split_lo(F + FFN_CHUNKS + 1, layer)
                gains(layer, q, (0,))
                ffn_residual(layer, F, 1)
                norm_los(layer, q, (0,))
                gains(layer, q, (1,))
                ffn_residual(layer, F, 2)
                norm_los(layer, q, (1,))
                ffn_residual(layer, F, 3)
                for i in (2, 3):
                    gains(layer, q, (i,))
                    norm_los(layer, q, (i,))

            def conv_taps(layer):
                dve.wait_ge(mid_hi, layer * 26 + 15)
                dve.wait_ge(padded, layer + 1)
                for m in range(CONV_K * KT):
                    tap, k = m // KT, m % KT
                    src = gluT[:, k, tap:tap + SEQ]
                    weight = vec[:, V_TAPS + tap, k:k + 1]
                    if tap == 0:
                        op = dve.tensor_scalar(yT[:, k, :], src, weight, vec[:, V_CONVB, k:k + 1], ALU.mult, ALU.add)
                    else:
                        dve.wait_ge(conv_step, layer * CONV_K * KT + m - KT + 1)
                        op = dve.scalar_tensor_tensor(yT[:, k, :], src, weight, yT[:, k, :], ALU.mult, ALU.add)
                    op.then_inc(conv_step, 1)
                    yield

            def win_unit(layer, w):
                bank, last = w % 3 * 2, WIN + 2 * w + 1
                if w < U_GATE:
                    if w:
                        dve.wait_ge(mid_T, layer * 26 + 11 + w)
                    gated_product(layer, 11 + w, bank)
                elif w < U_QK:
                    g = w - U_GATE
                    dest = gate_a if g < 2 else gate_b
                    if g == 0:
                        dve.wait_ge(bias_landed, 16 * layer + 16)
                    for t in range(TB):
                        unit_block(dve, layer, t, T_WIN + w, last)
                        dve.scalar_tensor_tensor(dest[:, t, cols(g % 2)], ps[:, bank + t, :], rstd[:, t:t + 1],
                                                 gate_bias[:, cols(g)], ALU.mult, ALU.add).then_inc(gate_pre, 1)

            def decay_scores(layer, hd):
                dve.wait_ge(score_done, layer * HEADS + hd + 1)
                dve.wait_ge(consts_late, 32)
                bank = 4 if hd else T0
                dve.tensor_tensor(scores[:, 0:SEQ], ps[:, bank, 0:SEQ], decay_sb[:, hd, :], ALU.mult)
                dve.tensor_tensor(scores[:, SEQ:3 * P], ps[:, bank, SEQ:3 * P], decay_sb[:, hd, 0:P], ALU.mult
                                  ).then_inc(decayed, 1)

            def head_outputs(layer, hd):
                dve.wait_ge(head_r, layer * HEADS + hd + 1)
                dve.wait_ge(unit_act, layer * 24 + 2 * (U_G - U_QK + hd) + 2)
                for t in range(TB):
                    dve.scalar_tensor_tensor(scaled[:, t, :], ps[:, 4 + t, :], r_head[:, t:t + 1],
                                             swish_g[:, t, hd * DV:(hd + 1) * DV], ALU.mult, ALU.mult
                                             ).then_inc(head_ready, 1)

            def head_los(layer, hd):
                for t in range(TB):
                    dve.wait_ge(head_hi, layer * 8 + 2 * hd + t + 1)
                    hi, lo = head_T_parts[hd % 2]
                    dve.tensor_tensor(lo[:, :, toks(t)], ps[:, T1 - t, :].rearrange("p (k t) -> p k t", k=4),
                                      hi[:, :, toks(t)].bitcast(F32), ALU.subtract).then_inc(head_lo, 1)

            def m_los(layer, pieces):
                for i in pieces:
                    n, t = half_of(i)
                    dve.wait_ge(m_hi, layer * 4 + i + 1)
                    dve.tensor_tensor(mT_lo[:, 4 * n:4 * n + 4, toks(t)],
                                      ps[:, T0 + i % 2, :].rearrange("p (k t) -> p k t", k=4),
                                      mT_hi[:, 4 * n:4 * n + 4, toks(t)].bitcast(F32), ALU.subtract
                                      ).then_inc(m_lo, 1)

            def conv_branch(layer, n):
                for t in range(TB):
                    unit_block(dve, layer, t, T_CONVO + n, CONVO + 2 * n + 1)
                    dve.tensor_tensor(gate_a[:, t, cols(n)], ps[:, (4, 0)[n] + t, :], gate_a[:, t, cols(n)], ALU.mult
                                      ).then_inc(conv_gated, 1)
                for t in range(TB):
                    dve.wait_ge(conv_gated, layer * 4 + 2 * n + t + 1)
                    dve.tensor_tensor(gate_a[:, t, cols(n)], gate_a[:, t, cols(n)], gate_b[:, t, cols(n)], ALU.add
                                      ).then_inc(m_ready, 1)

            done = [0]

            def step(op):
                done[0] += 1
                op.then_inc(start_step, 1)
                dve.wait_ge(start_step, done[0])

            for s in range(SLOTS):
                dve.sem_inc(lo_done[s], 1)
            dve.wait_ge(rope_in, 32)
            step(dve.tensor_copy(pos_f[:, :], pos_i[:, :]))
            for t in range(TB):
                step(dve.tensor_scalar(angle[:, t, :], inv_sb[:, :], pos_f[:, t:t + 1], None, ALU.mult))
            step(dve.tensor_scalar(turns[:, :, :], angle[:, :, :], 1.0 / TWO_PI, MAGIC, ALU.mult, ALU.add))
            step(dve.tensor_scalar(turns_c[:, :, :], angle[:, :, :], 1.0 / TWO_PI, 0.25, ALU.mult, ALU.add))
            step(dve.tensor_scalar(turns[:, :, :], turns[:, :, :], -MAGIC, None, ALU.add))
            step(dve.tensor_scalar(turns_c[:, :, :], turns_c[:, :, :], MAGIC, -MAGIC, ALU.add, ALU.add))
            for buf, keep in ((turns, 0), (turns_c, 1)):
                src = angle[:, :, :]
                for n, c in enumerate((C1, C2, C3)):
                    acc = junk[:, keep * 256:keep * 256 + 256].rearrange("p (t f) -> p t f", t=TB)
                    step(dve.scalar_tensor_tensor(acc, buf[:, :, :], -c, src, ALU.mult, ALU.add))
                    src = acc
                step(dve.tensor_scalar(acc, acc, TWO_PI / 4 if keep else 0.0, PI_IN, ALU.add, ALU.min))
                step(dve.tensor_scalar(buf[:, :, :], acc, -PI_IN, None, ALU.max))
            assert done[0] == ROPE_STEPS, done[0]
            dve.wait_ge(vec_landed, 16)
            split_lo(0, 0)
            for i in range(2):
                gains(0, N_FFN1, (i,))
                norm_los(0, N_FFN1, (i,))
            split_lo(1, 0)
            with dve.Fori(0, DEPTH) as layer:
                for i in (2, 3):
                    gains(layer, N_FFN1, (i,))
                    norm_los(layer, N_FFN1, (i,))
                ffn(layer, FFN1, 0)
                after_ffn(layer, FFN1, N_MIX)
                taps = None
                for u in range(WIN_UNITS):
                    if u:
                        win_unit(layer, u - 1)
                    if u == 18:
                        decay_scores(layer, 0)
                    if u == CONV_UNIT:
                        taps = conv_taps(layer)
                    for half, c in enumerate((ahead(WIN + 2 * u), ahead(WIN + 2 * u + 1))):
                        if c not in POOL_SPLITS:
                            split_lo(c, layer)
                        for _ in range(conv_steps(u)):
                            next(taps, None)
                        if u == 19 and not half:
                            head_outputs(layer, 0)
                head_los(layer, 0)
                for hd in range(HEADS):
                    if hd + 1 < HEADS:
                        decay_scores(layer, hd + 1)
                    if hd == 0:
                        for _ in taps:
                            pass
                    if hd == 3:
                        for n in range(2):
                            dve.wait_ge(ln_hi, layer * 2 + n + 1)
                            for t in range(TB):
                                part = (slice(None), slice(4 * n, 4 * n + 4), toks(t))
                                dve.tensor_tensor(uT_lo[part], yT[part], uT_hi[part].bitcast(F32), ALU.subtract
                                                  ).then_inc(convT_lo, 1)
                    split_lo(ahead(RET + 2 * hd), layer)
                    if hd == 1:
                        dve.wait_ge(mean_done, layer * 2 + 1)
                        for i in range(2):
                            part = yT[:, 4 * i:4 * i + 4, :]
                            dve.tensor_tensor(part, part, ps[:, T1, 0:SEQ].unsqueeze(1).to_broadcast([P, 4, SEQ]),
                                              ALU.subtract).then_inc(centred, 1)
                    if hd == 2:
                        dve.wait_ge(mean_done, layer * 2 + 2)
                        dve.tensor_scalar(acted[:, 0, :], ps[:, T1, 0:SEQ], EPS, None, ALU.add).then_inc(var_eps, 1)
                        dve.wait_ge(std_ready, layer + 1)
                        dve.reciprocal(acted[:, 0, :], acted[:, 0, :]).then_inc(ln_rstd, 1)
                        dve.wait_ge(ln_rstd, layer + 1)
                        for i in range(2):
                            part = yT[:, 4 * i:4 * i + 4, :]
                            dve.tensor_tensor(part, part, acted[:, 0, :].unsqueeze(1).to_broadcast([P, 4, SEQ]),
                                              ALU.mult).then_inc(normed, 1)
                    if hd + 1 < HEADS:
                        head_outputs(layer, hd + 1)
                    split_lo(ahead(RET + 2 * hd + 1), layer)
                    if hd + 1 < HEADS:
                        head_los(layer, hd + 1)
                for i in range(4):
                    n, t = half_of(i)
                    last_piece(dve, layer, i, P_RET, RET + 7)
                    dve.tensor_tensor(gate_b[:, t, cols(n)], ps[:, i, :], gate_b[:, t, cols(n)], ALU.mult
                                      ).then_inc(ret_gated, 1)
                split_lo(CONVO + 2, layer)
                split_lo(CONVO + 3, layer)
                conv_branch(layer, 0)
                split_lo(OUT, layer)
                m_los(layer, (0, 1))
                split_lo(OUT + 1, layer)
                conv_branch(layer, 1)
                split_lo(OUT + 2, layer)
                m_los(layer, (2, 3))
                split_lo(OUT + 3, layer)

                def out_residual(n):
                    for t in range(TB):
                        unit_block(dve, layer, t, T_OUT + n, OUT + 2 * n + 1)
                        dve.tensor_tensor(h[:, t, cols(n)], ps[:, (2, 0)[n] + t, :], h[:, t, cols(n)], ALU.add
                                          ).then_inc(h_ready, 1)

                out_residual(0)
                dve.wait_ge(p_hi, layer + 1)
                dve.tensor_tensor(hT_lo[:, 0:2, :], ps[:, T0, :].rearrange("p (k t) -> p k t", k=2),
                                  hT_hi[:, 0:2, :].bitcast(F32), ALU.subtract).then_inc(p_lo, 1)
                split_lo(FFN2 - 1, layer)
                gains(layer, N_FFN2, (0, 1))
                norm_los(layer, N_FFN2, (0, 1))
                split_lo(FFN2, layer)
                out_residual(1)
                for i in (2, 3):
                    gains(layer, N_FFN2, (i,))
                    norm_los(layer, N_FFN2, (i,))
                split_lo(PLEP, layer)
                ffn(layer, FFN2, 15)
                dve.wait_ge(ple_landed, 16 * layer + 16)
                after_ffn(layer, FFN2, N_PLE)
                split_lo(PG + 2, layer)
                split_lo(PG + 3, layer)
                with dve.If(DEPTH - 1 - layer):
                    split_lo(LAYER, layer)
                dve.wait_ge(e_normed, layer * TB + TB)
                for n in range(2):
                    for t in range(TB):
                        dve.wait_ge(pg_act, layer * 4 + 2 * n + t + 1)
                        dve.tensor_tensor(gate_b[:, t, cols(n)], gate_b[:, t, cols(n)], e_buf[:, t, cols(n)], ALU.mult
                                          ).then_inc(pg_prod, 1)
                    for t in range(TB):
                        dve.wait_ge(pg_prod, layer * 4 + 2 * n + t + 1)
                        dve.tensor_tensor(h[:, t, cols(n)], h[:, t, cols(n)], gate_b[:, t, cols(n)], ALU.add
                                          ).then_inc(h_ready, 1)
                    with dve.If(DEPTH - 1 - layer):
                        if n == 0:
                            dve.wait_ge(vec_landed, 16 * layer + 32)
                            gains(layer + 1, N_FFN1, (0, 1))
                            norm_los(layer + 1, N_FFN1, (0, 1))
                        else:
                            split_lo(LAYER + 1, layer)
            dve.wait_ge(rstd_ready, DEPTH * 4 + 1)
            for t in range(TB):
                dve.scalar_tensor_tensor(e_buf[:, t, :], h[:, t, :], rstd[:, t:t + 1], gain_f[:, :], ALU.mult, ALU.mult
                                         ).then_inc(out_ready, 1)

        @block.gpsimd
        def _(pool):
            def split_lo(c, layer):
                s = slot(c)
                pool.wait_ge(hi_done[s], nth(c, layer) + 1)
                pool.tensor_tensor(w_lo[:, s, :], raw[:, s, :], w_hi[:, s, :].bitcast(F32), ALU.subtract
                                   ).then_inc(lo_done[s], 1)

            def inverse_root(mean, with_eps, result, steps):
                pool.tensor_tensor(with_eps, mean, eps_tile, ALU.add).then_inc(pool_step, 1)
                pool.wait_ge(pool_step, steps + 1)
                return pool.tensor_tensor(result, with_eps, minus_half, ALU.pow)

            def norm_rstd(layer, q, steps):
                pool.wait_ge(ssq_ready, layer * 16 + q * 4 + 4)
                pool.tensor_tensor(ssq_sum, ssq[:, :, 0], ssq[:, :, 1], ALU.add).then_inc(pool_step, 1)
                pool.wait_ge(pool_step, steps + 1)
                inverse_root(ssq_sum, ms, rstd, steps + 1).then_inc(rstd_ready, 1)

            pool.memset(minus_half, -0.5).then_inc(preset, 1)
            pool.memset(eps_tile, EPS).then_inc(preset, 1)
            pool.memset(zero, 0.0).then_inc(preset, 1)
            pool.wait_ge(preset, 3)
            zeros = zero.unsqueeze(1).to_broadcast([P, KT, PAD])
            pool.wait_ge(trig, 2)
            with pool.Fori(0, DEPTH) as layer:
                steps = layer * POOL_STEPS
                pool.wait_ge(h_ready, layer * 16 + 4)
                pool.tensor_tensor(gluT[:, :, 0:PAD], zeros, zeros, ALU.add).then_inc(padded, 1)
                norm_rstd(layer, N_FFN1, steps)
                norm_rstd(layer, N_MIX, steps + 2)
                for c in POOL_SPLITS[:4]:
                    split_lo(c, layer)
                pool.wait_ge(gate_pre, layer * 8 + 8)
                for w in range(4):
                    pool.wait_ge(unit_act, layer * 24 + 2 * w + 2)
                    if w:
                        pool.wait_ge(qk_T, layer * 8 + 2 * w)
                    z = qk_in[:, w % 2]
                    t1, t2 = z[:, :, :, 0, :], z[:, :, :, 1, :]
                    cos = cos_sb[:, :, :].unsqueeze(2).to_broadcast([P, TB, 2, HALF])
                    sin = sin_sb[:, :, :].unsqueeze(2).to_broadcast([P, TB, 2, HALF])
                    pa, pb = prod_a[:, :, :, :], prod_b[:, :, :, :]
                    last = layer * 20 + 5 * w
                    pool.tensor_tensor(pa, t1, cos, ALU.mult).then_inc(rope_step, 1)
                    pool.tensor_tensor(pb, t2, sin, ALU.mult).then_inc(rope_step, 1)
                    pool.wait_ge(rope_step, last + 2)
                    pool.tensor_tensor(roped[:, :, :, 0, :], pa, pb, ALU.subtract).then_inc(rope_step, 1)
                    pool.wait_ge(rope_step, last + 3)
                    pool.tensor_tensor(pa, t2, cos, ALU.mult).then_inc(rope_step, 1)
                    pool.tensor_tensor(pb, t1, sin, ALU.mult).then_inc(rope_step, 1)
                    pool.wait_ge(rope_step, last + 5)
                    pool.tensor_tensor(roped[:, :, :, 1, :], pa, pb, ALU.add).then_inc(roped_ready, 1)
                for c in POOL_SPLITS[4:]:
                    split_lo(c, layer)
                for hd in range(HEADS):
                    pool.wait_ge(head_ssq, layer * 8 + 2 * hd + 2)
                    inverse_root(ssq_head, ms_head, r_head, steps + 4 + hd).then_inc(head_r, 1)
                norm_rstd(layer, N_FFN2, steps + 8)
                pool.wait_ge(e_squared, layer * 4 + 4)
                pool.tensor_tensor(ssq_e_sum, ssq_e[:, :, 0], ssq_e[:, :, 1], ALU.add).then_inc(pool_step, 1)
                pool.wait_ge(pool_step, steps + 11)
                inverse_root(ssq_e_sum, ms_e, r_e, steps + 11).then_inc(e_r, 1)
                norm_rstd(layer, N_PLE, steps + 12)
            norm_rstd(DEPTH, N_FFN1, DEPTH * POOL_STEPS)


def columns_chunks(w):
    return w.reshape(2, 4, P, COLS).transpose(0, 2, 1, 3).reshape(2, P, CHUNK)


def rows_chunks(w):
    return w.reshape(-1, 2, P, D).transpose(0, 2, 1, 3).reshape(-1, P, CHUNK)


def layer_chunks(i, w):
    def ffn(gate, up, down):
        down = rows_chunks(down)
        parts = []
        for k in range(FFN_UNITS):
            c = slice(256 * k, 256 * (k + 1))
            parts.append(columns_chunks(np.concatenate([gate[:, c], up[:, c]], axis=1)))
            if k:
                parts.append(down[k - 1:k])
        return parts + [down[-1:]]

    def units(m):
        return [columns_chunks(m[:, COLS * n:COLS * (n + 1)]) for n in range(m.shape[1] // COLS)]

    w_in = w["w_in"][i]
    conv_a, conv_b, q, k, v, g, gate_a, gate_b = np.split(w_in, np.cumsum([D, D, D, D, 2 * D, 2 * D, D]), axis=1)
    parts = ffn(w["ffn1_w_gate"][i], w["ffn1_w_up"][i], w["ffn1_w_down"][i])
    for n in range(4):
        c = slice(256 * n, 256 * (n + 1))
        parts.append(columns_chunks(np.concatenate([conv_b[:, c], conv_a[:, c]], axis=1)))
    for m in (gate_a, gate_b, q, k, v, g):
        parts += units(m)
    parts.append(rows_chunks(w["w_ret_o"][i]))
    parts += units(w["w_conv_o"][i]) + units(w["w_out"][i])
    first, *rest = ffn(w["ffn2_w_gate"][i], w["ffn2_w_up"][i], w["ffn2_w_down"][i])
    parts += [first, rows_chunks(w["w_ple_proj"][i])] + rest
    parts += units(w["w_ple_gate"][i])
    return parts


def shape_constants():
    f = np.float32
    log_g = np.log1p(-np.exp2(f(-5.0) - np.arange(HEADS, dtype=f))).astype(f)
    rel = (np.arange(SEQ, dtype=f)[None, :] - np.arange(P, dtype=f)[:, None])
    decay = np.where(rel >= 0, np.exp(log_g[:, None, None] * np.maximum(rel, f(0)), dtype=f), f(0))
    decay = (decay * f(DK ** -0.5)).astype(f).transpose(1, 0, 2)
    inv = np.power(f(ROPE_BASE), -np.arange(HALF, dtype=f) / f(HALF)).astype(f)
    return {
        "decay": np.ascontiguousarray(decay),
        "inv_freq": np.ascontiguousarray(np.broadcast_to(inv, (P, HALF))),
        "identity": np.eye(P, dtype=f),
        "mean_matrix": np.full((P, P), 1.0 / D, dtype=f),
    }


def kernel(**inputs):
    import concourse.bacc as bacc
    from concourse.bass_utils import run_bass_kernel_spmd

    w = {name: np.asarray(a) for name, a in inputs.items()}
    parts = [c for i in range(DEPTH) for c in layer_chunks(i, w)]
    names = ["ffn1_norm", "mix_norm", "ffn2_norm", "ple_norm", "conv_b", "conv_ln_g", "conv_ln_b"]
    vectors = np.concatenate([np.stack([w[n] for n in names], axis=1), w["conv_w"]], axis=1)
    vectors = np.concatenate([vectors, vectors[:1]], axis=0)
    arrays = {
        "stream": np.concatenate(parts, axis=0),
        "x": w["x"], "p": w["p"], "positions": w["positions"].reshape(TB, P).T,
        "vectors": np.ascontiguousarray(vectors.reshape(-1, KT, P).transpose(2, 0, 1)),
        "b_gates": w["b_gates"], "ple_gain": w["ple_proj_norm"], "final_gain": w["final_norm"],
        **shape_constants(),
    }
    nc = bacc.Bacc("TRN2", target_bir_lowering=False, num_devices=1)
    arrays = {f"in_{n}": np.ascontiguousarray(a) for n, a in arrays.items()}
    args = [nc.dram_tensor(n, a.shape, mybir.dt.from_np(a.dtype), kind="ExternalInput").ap() for n, a in arrays.items()]
    out = nc.dram_tensor("out", (1, SEQ, D), F32, kind="ExternalOutput").ap()
    build_kernel(nc, *args, out)
    return run_bass_kernel_spmd(nc, [arrays], core_ids=[0]).results[0]["out"]
```

```python
from contextlib import ExitStack

import numpy as np

import concourse.bass as bass
from concourse import mybir

ALU = mybir.AluOpType
ACT = mybir.ActivationFunctionType
F32 = mybir.dt.float32
F32R = mybir.dt.float32r
I32 = mybir.dt.int32

P = 128
DEPTH = 2
D = 1024
SEQ = 256
TB = SEQ // P
KT = D // P
D_FF = ((8 * D // 3 + 127) // 128) * 128
PLE = 256
CONV_K = 31
HEADS = 4
DK = D // HEADS
DV = 2 * D // HEADS
EPS = 1e-6
ROPE_BASE = 10000.0
HALF = DK // 2
COLS = 512
CHUNK = 2048
SLOTS = 3
FFN_UNITS = D_FF // 256

FFN1 = 0
FFN_CHUNKS = 3 * FFN_UNITS
WIN = FFN1 + FFN_CHUNKS
WIN_UNITS = 20
RET = WIN + 2 * WIN_UNITS + 1
CONVO = RET + 2 * HEADS + 1
OUT = CONVO + 4
FFN2 = OUT + 5
PLEP = FFN2 + 1
PG = FFN2 + FFN_CHUNKS
LAYER = PG + 4
EMPTY = (RET - 1, CONVO - 1)
CHUNKS = LAYER - len(EMPTY)
assert LAYER % SLOTS == 0

U_CONV, U_GATE, U_QK, U_V, U_G = 0, 4, 8, 12, 16

V_FFN1, V_MIX, V_FFN2, V_PLE, V_CONVB, V_LNG, V_LNB, V_TAPS = 0, 1, 2, 3, 4, 5, 6, 7
NVEC = 7 + CONV_K

N_FFN1, N_MIX, N_FFN2, N_PLE = range(4)
NORM_PIECES = 4 * 4
M_FFN1 = 0
M_GLU = M_FFN1 + FFN_UNITS
M_FFN2 = M_GLU + U_GATE - U_CONV
MIDS = M_FFN2 + FFN_UNITS
UNIT_ACTS = TB * (WIN_UNITS - U_QK)

MAGIC = 12582912.0
TWO_PI = 6.283185307179586
C1 = 6.28125
C2 = float(np.float32(TWO_PI - C1) - np.float32(np.float32(TWO_PI - C1) % np.float32(2.0 ** -20)))
C3 = TWO_PI - C1 - C2

PI_IN = 3.1415925
ROPE_STEPS = 17
POOL_STEPS = 14
POOL_SPLITS = tuple(WIN + n for n in (11, 13, 15, 17, 29, 31, 33, 35, 37, 39))
CONV_UNIT = 5


def conv_steps(u, half):
    if not CONV_UNIT <= u <= 18:
        return 0
    if u == 18 and half:
        return CONV_K * KT
    return 8 if u <= U_QK else 7 if u <= U_QK + 5 else 10 if u <= U_G else 9


def slot(c):
    return c % SLOTS


def nth(c, layer, j=0):
    empty = [e for e in EMPTY if slot(e) == slot(c)]
    return layer * (LAYER // SLOTS - len(empty)) + c // SLOTS - sum(e < c for e in empty) + j


def ahead(c):
    for _ in range(2):
        c += 2 if c + 1 in EMPTY else 1
    return c


def build_kernel(nc, stream, x, p, positions, vectors, b_gates, ple_gain, final_gain,
                 decay, inv_freq, identity, mean_matrix, out):
    ctx = ExitStack()
    with ctx:
        def sem(name):
            return ctx.enter_context(nc.semaphore(name))

        top = [-(-nc.sbuf_base // 32) * 32]

        def at(name, shape, dt=F32, offset=None):
            n = 4 * int(np.prod(shape[1:]))
            o = top[0] if offset is None else offset
            if offset is None:
                top[0] += n
            return nc.alloc_sbuf_tensor_at(name, shape, dt, offset=o), o

        raw, _ = at("raw", [P, SLOTS, CHUNK])
        w_hi, _ = at("w_hi", [P, SLOTS, CHUNK], F32R)
        w_lo, _ = at("w_lo", [P, SLOTS, CHUNK], F32R)
        h, _ = at("h", [P, TB, D])
        uT_hi, _ = at("uT_hi", [P, KT, SEQ], F32R)
        uT_lo, o_uT_lo = at("uT_lo", [P, KT, SEQ], F32R)
        centred_sq, _ = at("centred_sq", [P, KT, SEQ], offset=o_uT_lo)
        gate_a, _ = at("gate_a", [P, TB, D])
        gate_b, _ = at("gate_b", [P, TB, D])
        v, o_v = at("v", [P, TB, HEADS * DV])
        mT_hi, _ = at("mT_hi", [P, KT, SEQ], F32R, offset=o_v)
        mT_lo, _ = at("mT_lo", [P, KT, SEQ], F32R, offset=o_v + 8192)
        swish_g, o_sg = at("swish_g", [P, TB, HEADS * DV])
        gate_bias, _ = at("gate_bias", [P, 2 * D], offset=o_sg)
        roped, _ = at("roped", [P, TB, 2, 2, HALF], offset=o_sg)
        prod_a, _ = at("prod_a", [P, TB, 2, HALF], offset=o_sg + 4096)
        prod_b, _ = at("prod_b", [P, TB, 2, HALF], offset=o_sg + 6144)
        qk_in, _ = at("qk_in", [P, 2, TB, 2, 2, HALF], offset=o_sg + 8192)
        qT, o_qT = at("qT", [P, KT, SEQ])
        kT, o_kT = at("kT", [P, KT, SEQ])
        e_buf, _ = at("e_buf", [P, TB, D], offset=o_qT)
        gain_e, _ = at("gain_e", [P, D], offset=o_kT)
        gain_f, _ = at("gain_f", [P, D], offset=o_kT + 4096)
        PAD = CONV_K - 1
        gluT, o_gluT = at("gluT", [P, KT, PAD + SEQ])
        oT_hi, _ = at("oT_hi", [P, 4, SEQ], F32R, offset=o_gluT)
        oT_lo, _ = at("oT_lo", [P, 4, SEQ], F32R, offset=o_gluT + 4096)
        yT, o_yT = at("yT", [P, KT, SEQ])
        p_in, _ = at("p_in", [P, TB, PLE], offset=o_yT)
        hT_hi, _ = at("hT_hi", [P, 4, SEQ], F32R)
        hT_lo, _ = at("hT_lo", [P, 4, SEQ], F32R)
        scaled, _ = at("scaled", [P, 2, 4 * P])
        acted, _ = at("acted", [P, TB, 256])
        mid, _ = at("mid", [P, TB, 256])
        junk, _ = at("junk", [P, COLS])
        scores, _ = at("scores", [P, 3 * P])
        decay_sb, _ = at("decay_sb", [P, HEADS, SEQ])
        cos_sb, _ = at("cos_sb", [P, TB, HALF])
        sin_sb, _ = at("sin_sb", [P, TB, HALF])
        ident, _ = at("ident", [P, P])
        means, _ = at("means", [P, P])
        vec, _ = at("vec", [P, NVEC, KT])
        vec_ple, _ = at("vec_ple", [P, KT])
        small, _ = at("small", [P, 64])
        angle, _ = at("angle", [P, TB, HALF], offset=o_v)
        turns, _ = at("turns", [P, TB, HALF], offset=o_v + 1024)
        turns_c, _ = at("turns_c", [P, TB, HALF], offset=o_v + 2048)
        inv_sb, _ = at("inv_sb", [P, HALF], offset=o_v + 3072)
        pos_i, _ = at("pos_i", [P, TB], I32, offset=o_v + 4096)
        pos_f, _ = at("pos_f", [P, TB], offset=o_v + 4128)
        assert top[0] <= nc.sbuf_usable_end, top[0]

        channel_std, channel_mean = acted[:, 0, :], acted[:, 1, :]
        ssq = small[:, 0:4].rearrange("p (t n) -> p t n", t=TB)
        ms = small[:, 4:6]
        rstd = small[:, 6:8]
        ssq_head = small[:, 8:10]
        ms_head = small[:, 10:12]
        r_head = small[:, 12:14]
        ssq_e = small[:, 14:18].rearrange("p (t n) -> p t n", t=TB)
        ms_e = small[:, 18:20]
        r_e = small[:, 20:22]
        minus_half = small[:, 22:24]
        eps_tile = small[:, 28:30]
        zero = small[:, 30:31]
        ssq_sum = small[:, 24:26]
        ssq_e_sum = small[:, 26:28]

        ps = ctx.enter_context(nc.psum_tensor("ps", [P, 8, COLS], F32))
        T0, T1 = 6, 7

        landed = [sem(f"landed{s}") for s in range(SLOTS)]
        hi_done = [sem(f"hi_done{s}") for s in range(SLOTS)]
        lo_done = [sem(f"lo_done{s}") for s in range(SLOTS)]
        used = [sem(f"used{s}") for s in range(SLOTS)]
        tb0_done = sem("tb0_done")
        piece_done = sem("piece_done")
        h_ready = sem("h_ready")
        norm_T = sem("norm_T")
        norm_g = sem("norm_g")
        norm_hi = sem("norm_hi")
        norm_lo = sem("norm_lo")
        ssq_ready = sem("ssq_ready")
        rstd_ready = sem("rstd_ready")
        acted_ready = sem("acted_ready")
        mid_ready = sem("mid_ready")
        mid_T = sem("mid_T")
        mid_hi = sem("mid_hi")
        mid_lo = sem("mid_lo")
        unit_act = sem("unit_act")
        gate_pre = sem("gate_pre")
        gate_act = sem("gate_act")
        roped_ready = sem("roped_ready")
        rope_step = sem("rope_step")
        qk_T = sem("qk_T")
        qk_evac = sem("qk_evac")
        conv_step = sem("conv_step")
        mean_done = sem("mean_done")
        mean_copied = sem("mean_copied")
        centred = sem("centred")
        squared = sem("squared")
        tile_sum = sem("tile_sum")
        std_ready = sem("std_ready")
        ln_rstd = sem("ln_rstd")
        normed = sem("normed")
        ln_silu = sem("ln_silu")
        ln_hi = sem("ln_hi")
        convT_lo = sem("convT_lo")
        score_done = sem("score_done")
        decayed = sem("decayed")
        pv_done = sem("pv_done")
        head_ssq = sem("head_ssq")
        head_r = sem("head_r")
        head_ready = sem("head_ready")
        head_T = sem("head_T")
        head_hi = sem("head_hi")
        head_lo = sem("head_lo")
        ret_gated = sem("ret_gated")
        conv_gated = sem("conv_gated")
        m_ready = sem("m_ready")
        m_T = sem("m_T")
        m_hi = sem("m_hi")
        m_lo = sem("m_lo")
        p_T = sem("p_T")
        p_hi = sem("p_hi")
        p_lo = sem("p_lo")
        e_squared = sem("e_squared")
        e_evac = sem("e_evac")
        e_r = sem("e_r")
        e_normed = sem("e_normed")
        pg_act = sem("pg_act")
        pg_prod = sem("pg_prod")
        pool_step = sem("pool_step")
        consts = sem("consts")
        consts_late = sem("consts_late")
        rope_in = sem("rope_in")
        x_landed = [sem(f"x_landed{n}") for n in range(2)]
        vec_landed = sem("vec_landed")
        ple_landed = sem("ple_landed")
        bias_landed = sem("bias_landed")
        p_landed = sem("p_landed")
        gain_landed = sem("gain_landed")
        start_step = sem("start_step")
        trig = sem("trig")
        padded = sem("padded")
        preset = sem("preset")
        out_ready = sem("out_ready")
        stored = sem("stored")

        head_T_parts = ((hT_hi, hT_lo), (oT_hi, oT_lo))

        def half_of(i):
            return i // TB, i % TB

        def cols(n):
            return slice(n * COLS, (n + 1) * COLS)

        def toks(t):
            return slice(t * P, (t + 1) * P)

        block = ctx.enter_context(nc.Block())

        @block.sync
        def _(sp):
            def load(c, layer, j=0):
                sp.wait_ge(lo_done[slot(c)], nth(c, layer, j) + 1)
                number = layer * CHUNKS + SLOTS * j + c - sum(e < c for e in EMPTY)
                sp.dma_start(raw[:, slot(c), :], stream[bass.ds(number, 1), :, :].rearrange("a p n -> p (a n)")
                             ).then_inc(landed[slot(c)], 16)

            sp.dma_start(inv_sb[:, :], inv_freq).then_inc(rope_in, 16)
            sp.dma_start(ident[:, :], identity).then_inc(consts, 16)
            with sp.Fori(0, DEPTH) as layer:
                for first, last in ((0, EMPTY[0]), (EMPTY[0] + 1, EMPTY[1]), (EMPTY[1] + 1, LAYER)):
                    rounds, rest = divmod(last - first, SLOTS)
                    with sp.Fori(0, rounds) as j:
                        for c in range(first, first + SLOTS):
                            load(c, layer, j)
                    for c in range(last - rest, last):
                        load(c, layer)
            for t in range(TB):
                for n in range(2):
                    sp.wait_ge(out_ready, 2 * t + n + 1)
                    sp.dma_start(out[0, toks(t), cols(n)], e_buf[:, t, cols(n)]).then_inc(stored, 16)
            sp.wait_ge(stored, 2 * 16 * TB)

        @block.tensor
        def _(pe):
            def product(bank, lhs_hi, lhs_lo, kts, t, c, first, last, col=None):
                s = slot(c)
                steps = []
                for i, kt in enumerate(kts):
                    rows = slice(i * COLS, (i + 1) * COLS) if col is None else slice(i * D + col, i * D + col + COLS)
                    for a, b in ((lhs_hi, w_hi), (lhs_hi, w_lo), (lhs_lo, w_hi)):
                        steps.append((a[:, kt, toks(t)], b[:, s, rows]))
                for n, (a, b) in enumerate(steps):
                    mm = pe.matmul(ps[:, bank, :], a, b, start=first and n == 0, stop=last and n == len(steps) - 1)
                return mm

            def half_unit(c, layer, banks, lhs_hi, lhs_lo, second, j=0, before=(), between=()):
                pe.wait_ge(lo_done[slot(c)], nth(c, layer, j) + 2)
                kts = range(4, 8) if second else range(4)
                for t in range(TB):
                    if before:
                        pe.wait_ge(before[0], before[1] + t)
                    mm = product(banks[t], lhs_hi, lhs_lo, kts, t, c, not second, second)
                    if t == 1:
                        mm.then_inc(used[slot(c)], 1)
                    elif second:
                        mm.then_inc(tb0_done, 1)
                    if t == 0:
                        for do in between:
                            do()

            def first_unit(c, layer, banks, lhs_hi, lhs_lo, ready, pieces, rest):
                half_unit(c, layer, banks, lhs_hi, lhs_lo, False, before=(ready, pieces + 1), between=(rest,))
                half_unit(c + 1, layer, banks, lhs_hi, lhs_lo, True, before=(ready, pieces + 3))

            def rows_chunk(c, layer, lhs, kts, first, last, j=0, after=None, before=None):
                pe.wait_ge(lo_done[slot(c)], nth(c, layer, j) + 2)
                for i in range(4):
                    n, t = half_of(i)
                    if before and i in before:
                        pe.wait_ge(*before[i])
                    mm = product(i, *lhs, kts, t, c, first, last, col=n * COLS)
                    if i == 3:
                        mm.then_inc(used[slot(c)], 1)
                    elif last:
                        mm.then_inc(piece_done, 1)
                    if after and i in after:
                        after[i]()

            def transpose4(bank, pieces):
                for n, a in enumerate(pieces):
                    mm = pe.transpose(ps[:, bank, n * P:(n + 1) * P], a, ident[:, :])
                return mm

            def norm_transposes(layer, q, pieces=range(4)):
                for i in pieces:
                    n, t = half_of(i)
                    pe.wait_ge(h_ready, layer * NORM_PIECES + q * 4 + i + 1)
                    if i >= 2:
                        pe.wait_ge(norm_g, layer * NORM_PIECES + q * 4 + i - 1)
                    transpose4(T0 + i % 2, [h[:, t, n * COLS + k * P:n * COLS + (k + 1) * P] for k in range(4)]
                               ).then_inc(norm_T, 1)

            def mid_transposes(layer, n):
                pe.wait_ge(mid_ready, layer * 2 * MIDS + 2 * n + 2)
                transpose4(T0, [mid[:, t, k * P:(k + 1) * P] for k in range(2) for t in range(TB)]
                           ).then_inc(mid_T, 1)

            def ffn(layer, F, q, mids, next_q):
                hT = (hT_hi, hT_lo)

                def down(c, j, kts=range(2), first=False, last=False, unit=0, after=None):
                    pe.wait_ge(mid_lo, layer * 2 * FFN_UNITS + (FFN_UNITS if F else 0) + unit + j + 1)
                    rows_chunk(c, layer, hT, kts, first, last, j=j, after=after)

                first_unit(F - 1 if F else F, layer, (4, 5) if F else (2, 3), uT_hi, uT_lo, norm_lo, layer * NORM_PIECES + q * 4,
                           lambda: norm_transposes(layer, q, (2, 3)))
                if F:
                    rows_chunk(PLEP, layer, (hT_hi, hT_lo), range(2), True, True)
                    mid_transposes(layer, mids)
                half_unit(F + 2, layer, (4, 5), uT_hi, uT_lo, False)
                if not F:
                    mid_transposes(layer, mids)
                half_unit(F + 3, layer, (4, 5), uT_hi, uT_lo, True)
                if F:
                    pe.wait_ge(e_evac, layer * 4 + 4)
                down(F + 4, 0, first=True)
                mid_transposes(layer, mids + 1)
                with pe.Fori(1, FFN_UNITS - 2) as j:
                    half_unit(F + 2, layer, (4, 5), uT_hi, uT_lo, False, j=j)
                    half_unit(F + 3, layer, (4, 5), uT_hi, uT_lo, True, j=j)
                    down(F + 4, j)
                    mid_transposes(layer, mids + 1 + j)
                j = FFN_UNITS - 2
                half_unit(F + 2, layer, (4, 5), uT_hi, uT_lo, False, j=j)
                half_unit(F + 3, layer, (4, 5), uT_hi, uT_lo, True, j=j)
                down(F + 4, j, after={1: lambda: mid_transposes(layer, mids + 1 + j)})
                down(F + FFN_CHUNKS - 1, 0, kts=range(2, 4), last=True, unit=FFN_UNITS - 1,
                     after={1: lambda: norm_transposes(layer, next_q, (0,)),
                            2: lambda: norm_transposes(layer, next_q, (1,))})

            def head_scores(layer, hd):
                bank = 4 if hd else T0
                pe.wait_ge(qk_evac, layer * 8 + 8)
                for k in range(2):
                    pe.matmul(ps[:, bank, 0:SEQ], kT[:, 2 * hd + k, 0:P], qT[:, 2 * hd + k, :],
                              start=k == 0, stop=k == 1)
                for k in range(2):
                    mm = pe.matmul(ps[:, bank, SEQ:SEQ + P], kT[:, 2 * hd + k, P:SEQ], qT[:, 2 * hd + k, P:SEQ],
                                   start=k == 0, stop=k == 1)
                mm.then_inc(score_done, 1)

            def head_values(layer, hd):
                pe.wait_ge(decayed, layer * HEADS + hd + 1)
                cv = slice(hd * DV, (hd + 1) * DV)
                pe.matmul(ps[:, 4, :], scores[:, 0:P], v[:, 0, cv], start=True, stop=True).then_inc(pv_done, 1)
                pe.matmul(ps[:, 5, :], scores[:, P:SEQ], v[:, 0, cv], start=True, stop=False)
                pe.matmul(ps[:, 5, :], scores[:, SEQ:3 * P], v[:, 1, cv], start=False, stop=True).then_inc(pv_done, 1)

            def head_transposes(layer, hd):
                for t in range(TB):
                    pe.wait_ge(head_ready, layer * 8 + 2 * hd + t + 1)
                    transpose4(T1 - t, [scaled[:, t, k * P:(k + 1) * P] for k in range(4)]).then_inc(head_T, 1)

            def m_transposes(layer, pieces):
                for i in pieces:
                    n, t = half_of(i)
                    pe.wait_ge(m_ready, layer * 4 + i + 1)
                    if i >= 2:
                        pe.wait_ge(m_lo, layer * 4 + i - 1)
                    transpose4(T0 + i % 2, [gate_a[:, t, n * COLS + k * P:n * COLS + (k + 1) * P] for k in range(4)]
                               ).then_inc(m_T, 1)

            def warm_up(times):
                for _ in range(times):
                    pe.transpose(ps[:, 5, 0:P], ident[:, :], ident[:, :])

            for s in range(SLOTS):
                pe.sem_inc(used[s], 1)
            pe.wait_ge(consts, 16)
            warm_up(31)
            pe.wait_ge(x_landed[0], 16)
            pe.sem_inc(h_ready, 2)
            norm_transposes(0, N_FFN1, (0, 1))
            warm_up(34)
            pe.wait_ge(x_landed[1], 16)
            pe.sem_inc(h_ready, 2)
            with pe.Fori(0, DEPTH) as layer:
                ffn(layer, FFN1, N_FFN1, M_FFN1, N_MIX)
                for u in range(WIN_UNITS):
                    banks = (u % 3 * 2, u % 3 * 2 + 1)
                    w = u - 3
                    if U_CONV <= w < U_GATE:
                        pe.wait_ge(mid_ready, layer * 2 * MIDS + 2 * M_GLU + 2 * w + 2)
                    elif U_GATE <= w < U_QK:
                        pe.wait_ge(gate_pre, layer * 8 + 2 * (w - U_GATE) + 2)
                    elif U_QK <= w:
                        pe.wait_ge(unit_act, layer * UNIT_ACTS + 2 * (w - U_QK) + 2)
                    if u == 0:
                        first_unit(WIN, layer, banks, uT_hi, uT_lo, norm_lo, layer * NORM_PIECES + N_MIX * 4,
                                   lambda: norm_transposes(layer, N_MIX, (2, 3)))
                    else:
                        half_unit(WIN + 2 * u, layer, banks, uT_hi, uT_lo, False)
                        half_unit(WIN + 2 * u + 1, layer, banks, uT_hi, uT_lo, True)
                    if U_CONV < u <= U_GATE:
                        if u - 1 > U_CONV:
                            pe.wait_ge(mid_hi, layer * MIDS + M_GLU + u - 1)
                        mid_transposes(layer, M_GLU + u - 1)
                    if U_QK + 2 <= u < U_QK + 6:
                        w = u - 2 - U_QK
                        pe.wait_ge(roped_ready, layer * 4 + w + 1)
                        for t in range(TB):
                            if w:
                                pe.wait_ge(qk_evac, layer * 8 + 2 * (w - 1) + t + 1)
                            transpose4(T0 + t, [roped[:, t, k // 2, k % 2, :] for k in range(4)]).then_inc(qk_T, 1)
                    if u == 17:
                        head_scores(layer, 0)
                    if u == 18:
                        pe.wait_ge(unit_act, layer * UNIT_ACTS + 2 * (17 - U_QK) + 2)
                        head_values(layer, 0)
                    if u == 19:
                        head_transposes(layer, 0)
                        head_scores(layer, 1)
                pe.wait_ge(unit_act, layer * UNIT_ACTS + UNIT_ACTS - 2)
                for hd in range(HEADS):
                    if hd == 2:
                        pe.wait_ge(head_lo, layer * 8 + 2 * hd + 1)
                        pe.wait_ge(tile_sum, layer * 6 + 6)
                        pe.matmul(ps[:, T1, 0:SEQ], means[:, :], centred_sq[:, 0, :], start=True, stop=True
                                  ).then_inc(mean_done, 1)
                    lhs = head_T_parts[hd % 2]
                    more = hd + 1 < HEADS

                    def next_values():
                        head_values(layer, hd + 1)
                        if hd == 0:
                            pe.wait_ge(unit_act, layer * UNIT_ACTS + UNIT_ACTS)

                    def next_transposes():
                        if hd == 0:
                            pe.wait_ge(mean_copied, layer + 1)
                        if hd == 2:
                            pe.wait_ge(std_ready, layer + 1)
                        head_transposes(layer, hd + 1)
                        if hd + 2 < HEADS:
                            head_scores(layer, hd + 2)

                    rows_chunk(RET + 2 * hd, layer, lhs, range(2), hd == 0, False,
                               before={t: (head_lo, layer * 8 + 2 * hd + t + 1) for t in range(TB)},
                               after={1: next_values} if more else None)
                    if hd == 0:
                        pe.wait_ge(consts_late, 32)
                        pe.wait_ge(tile_sum, layer * 6 + 3)
                        pe.matmul(ps[:, T1, 0:SEQ], means[:, :], centred_sq[:, 0, :], start=True, stop=True
                                  ).then_inc(mean_done, 1)
                    rows_chunk(RET + 2 * hd + 1, layer, lhs, range(2, 4), False, not more,
                               after={1: next_transposes} if more else None)
                half_unit(CONVO, layer, (4, 5), uT_hi, uT_lo, False, before=(convT_lo, layer * 4 + 1))
                half_unit(CONVO + 1, layer, (4, 5), uT_hi, uT_lo, True, before=(convT_lo, layer * 4 + 3))
                pe.wait_ge(ret_gated, layer * 4 + 2)
                half_unit(CONVO + 2, layer, (0, 1), uT_hi, uT_lo, False)
                m_transposes(layer, (0, 1))
                half_unit(CONVO + 3, layer, (0, 1), uT_hi, uT_lo, True)
                pe.wait_ge(ret_gated, layer * 4 + 4)
                first_unit(OUT, layer, (2, 3), mT_hi, mT_lo, m_lo, layer * 4, lambda: m_transposes(layer, (2, 3)))
                pe.wait_ge(p_landed, layer * 16 + 16)
                transpose4(T0, [p_in[:, t, k * P:(k + 1) * P] for k in range(2) for t in range(TB)]).then_inc(p_T, 1)
                half_unit(OUT + 2, layer, (0, 1), mT_hi, mT_lo, False)
                pe.wait_ge(p_lo, layer + 1)
                norm_transposes(layer, N_FFN2, (0,))
                norm_transposes(layer, N_FFN2, (1,))
                half_unit(OUT + 3, layer, (0, 1), mT_hi, mT_lo, True)
                ffn(layer, FFN2, N_FFN2, M_FFN2, N_PLE)
                first_unit(PG, layer, (4, 5), uT_hi, uT_lo, norm_lo, layer * NORM_PIECES + N_PLE * 4,
                           lambda: norm_transposes(layer, N_PLE, (2, 3)))
                half_unit(PG + 2, layer, (0, 1), uT_hi, uT_lo, False)

                def next_norm():
                    with pe.If(DEPTH - 1 - layer):
                        norm_transposes(layer + 1, N_FFN1, (0, 1))

                half_unit(PG + 3, layer, (0, 1), uT_hi, uT_lo, True, between=(next_norm,))

        T_FFN1 = 0
        T_WIN = T_FFN1 + FFN_UNITS
        T_CONVO = T_WIN + WIN_UNITS
        T_OUT = T_CONVO + 2
        T_FFN2 = T_OUT + 2
        T_PG = T_FFN2 + FFN_UNITS
        T_LAYER = T_PG + 2
        P_FFN1, P_RET, P_E, P_FFN2, P_LAYER = 0, 3, 6, 9, 12

        def unit_block(eng, layer, t, first_index, last_chunk, j=0, k=0):
            if t == 0:
                eng.wait_ge(tb0_done, layer * T_LAYER + first_index + k + 1)
            else:
                eng.wait_ge(used[slot(last_chunk)], nth(last_chunk, layer, j) + 2)

        def last_piece(eng, layer, i, first_index, last_chunk):
            if i < 3:
                eng.wait_ge(piece_done, layer * P_LAYER + first_index + i + 1)
            else:
                eng.wait_ge(used[slot(last_chunk)], nth(last_chunk, layer) + 2)

        @block.scalar
        def _(act):
            def split_hi(c, layer, j=0):
                s = slot(c)
                act.wait_ge(landed[s], 16 * (nth(c, layer, j) + 1))
                act.wait_ge(used[s], nth(c, layer, j) + 1)
                act.activation(w_hi[:, s, :], raw[:, s, :], ACT.Copy).then_inc(hi_done[s], 1)

            def norm_his(layer, q, pieces):
                for i in pieces:
                    n, t = half_of(i)
                    act.wait_ge(norm_g, layer * NORM_PIECES + q * 4 + i + 1)
                    act.activation(uT_hi[:, 4 * n:4 * n + 4, toks(t)],
                                   scaled[:, i % 2, :].rearrange("p (k t) -> p k t", k=4),
                                   ACT.Copy).then_inc(norm_hi, 1)

            def squares(layer, q, pieces=range(4)):
                for i in pieces:
                    n, t = half_of(i)
                    act.wait_ge(h_ready, layer * NORM_PIECES + q * 4 + i + 1)
                    if i:
                        act.wait_ge(ssq_ready, layer * NORM_PIECES + q * 4 + i)
                    act.activation(junk[:, :], h[:, t, cols(n)], ACT.Square, scale=D ** -0.5,
                                   accum_out=ssq[:, t, n:n + 1]).then_inc(ssq_ready, 1)

            def gated(layer, n, func, first_index, last_chunk, j=0, k=0):
                for t in range(TB):
                    unit_block(act, layer, t, first_index, last_chunk, j, k)
                    act.activation(acted[:, t, :], ps[:, n + t, 0:256], func, scale=rstd[:, t:t + 1]
                                   ).then_inc(acted_ready, 1)

            def ffn(layer, F, q, mids, first_index):
                def mid_upper(k, to=0):
                    act.wait_ge(mid_T, layer * MIDS + mids + k + 1)
                    act.activation(hT_hi[:, to:to + 2, :], ps[:, T0, :].rearrange("p (k t) -> p k t", k=2),
                                   ACT.Copy).then_inc(mid_hi, 1)

                first_last = FFN2 if F else FFN1 + 1
                act.wait_ge(rstd_ready, layer * 4 + q + 1)
                gated(layer, 4 if F else 2, ACT.Silu, first_index, first_last)
                split_hi(F + 3, layer)
                if F:
                    for i in range(4):
                        n, t = half_of(i)
                        last_piece(act, layer, i, P_E, PLEP)
                        act.activation(e_buf[:, t, cols(n)], ps[:, i, :], ACT.Copy).then_inc(e_evac, 1)

                def unit(j, first=False):
                    mid_upper(j)
                    if F and first:
                        for i in range(4):
                            n, t = half_of(i)
                            act.wait_ge(e_evac, layer * 4 + i + 1)
                            if i:
                                act.wait_ge(e_squared, layer * 4 + i)
                            else:
                                act.wait_ge(ssq_ready, layer * NORM_PIECES + N_FFN2 * 4 + 4)
                            act.activation(junk[:, :], e_buf[:, t, cols(n)], ACT.Square, scale=D ** -0.5,
                                           accum_out=ssq_e[:, t, n:n + 1]).then_inc(e_squared, 1)
                        act.wait_ge(e_squared, layer * 4 + 4)
                    split_hi(F + 4, layer, j)
                    split_hi(F + 5, layer, j)
                    gated(layer, 4, ACT.Silu, first_index + 1, F + 3, j, j)
                    split_hi(F + 6, layer, j)

                unit(0, True)
                with act.Fori(1, FFN_UNITS - 1) as j:
                    unit(j)
                mid_upper(FFN_UNITS - 1, 2)
                act.preload_act_table(ACT.Sigmoid)
                split_hi(F + FFN_CHUNKS + 1, layer)

            def head_squares(layer, hd):
                for t in range(TB):
                    act.wait_ge(pv_done, layer * 8 + 2 * hd + t + 1)
                    if t:
                        act.wait_ge(head_ssq, layer * 8 + 2 * hd + t)
                    act.activation(junk[:, :], ps[:, 4 + t, :], ACT.Square, scale=DV ** -0.5,
                                   accum_out=ssq_head[:, t:t + 1]).then_inc(head_ssq, 1)

            def head_his(layer, hd):
                if hd == 1:
                    act.wait_ge(conv_step, (layer + 1) * CONV_K * KT)
                for t in range(TB):
                    act.wait_ge(head_T, layer * 8 + 2 * hd + t + 1)
                    hi, _ = head_T_parts[hd % 2]
                    act.activation(hi[:, :, toks(t)], ps[:, T1 - t, :].rearrange("p (k t) -> p k t", k=4), ACT.Copy
                                   ).then_inc(head_hi, 1)

            def m_his(layer, pieces):
                for i in pieces:
                    n, t = half_of(i)
                    act.wait_ge(m_T, layer * 4 + i + 1)
                    act.activation(mT_hi[:, 4 * n:4 * n + 4, toks(t)],
                                   ps[:, T0 + i % 2, :].rearrange("p (k t) -> p k t", k=4),
                                   ACT.Copy).then_inc(m_hi, 1)

            def glu_copy(layer, w):
                act.wait_ge(mid_T, layer * MIDS + M_GLU + w + 1)
                act.activation(gluT[:, 2 * w:2 * w + 2, PAD:PAD + SEQ],
                               ps[:, T0, :].rearrange("p (k t) -> p k t", k=2), ACT.Copy).then_inc(mid_hi, 1)

            def qk_copy(layer, w):
                dest = qT if w < 2 else kT
                for t in range(TB):
                    act.wait_ge(qk_T, layer * 8 + 2 * w + t + 1)
                    act.activation(dest[:, 4 * (w % 2):4 * (w % 2) + 4, toks(t)],
                                   ps[:, T0 + t, :].rearrange("p (k t) -> p k t", k=4), ACT.Copy).then_inc(qk_evac, 1)

            def win_unit(layer, w):
                bank, last = w % 3 * 2, WIN + 2 * w + 1
                if w < U_GATE:
                    if w:
                        act.wait_ge(mid_ready, layer * 2 * MIDS + 2 * M_GLU + 2 * w)
                    gated(layer, bank, ACT.Sigmoid, T_WIN + w, last)
                    if w:
                        glu_copy(layer, w - 1)
                elif w < U_QK:
                    g = w - U_GATE
                    dest = gate_a if g < 2 else gate_b
                    if g == 0:
                        glu_copy(layer, U_GATE - 1)
                    act.wait_ge(gate_pre, layer * 8 + 2 * g + 2)
                    act.activation(dest[:, :, cols(g % 2)], dest[:, :, cols(g % 2)], ACT.Sigmoid).then_inc(gate_act, 1)
                elif w < U_V:
                    r = w - U_QK
                    if r >= 2:
                        act.wait_ge(roped_ready, layer * 4 + r - 1)
                    for t in range(TB):
                        unit_block(act, layer, t, T_WIN + w, last)
                        act.activation(qk_in[:, r % 2, t].rearrange("p h a c -> p (h a c)"), ps[:, bank + t, :],
                                       ACT.Copy, scale=rstd[:, t:t + 1]).then_inc(unit_act, 1)
                elif w < U_G:
                    for t in range(TB):
                        unit_block(act, layer, t, T_WIN + w, last)
                        act.activation(v[:, t, cols(w - U_V)], ps[:, bank + t, :], ACT.Copy,
                                       scale=rstd[:, t:t + 1]).then_inc(unit_act, 1)
                else:
                    for t in range(TB):
                        unit_block(act, layer, t, T_WIN + w, last)
                        act.activation(swish_g[:, t, cols(w - U_G)], ps[:, bank + t, :], ACT.Silu,
                                       scale=rstd[:, t:t + 1]).then_inc(unit_act, 1)
                if U_QK + 2 <= w < U_QK + 6:
                    qk_copy(layer, w - U_QK - 2)

            act.dma_start(pos_i[:, :], positions).then_inc(rope_in, 16)
            act.dma_start(vec[:, :, :], vectors[:, 0:NVEC, :]).then_inc(vec_landed, 16)
            for n in range(2):
                act.dma_start(h[:, :, cols(n)], x[:, :, cols(n)].rearrange("b (t p) d -> p (b t) d", p=P)
                              ).then_inc(x_landed[n], 16)
            act.dma_start(means[:, :], mean_matrix).then_inc(consts_late, 16)
            act.dma_start(decay_sb[:, :, :], decay).then_inc(consts_late, 16)
            act.preload_act_table(ACT.Silu)
            act.wait_ge(preset, 3)
            split_hi(0, 0)
            norm_his(0, N_FFN1, (0,))
            split_hi(1, 0)
            norm_his(0, N_FFN1, (1,))
            squares(0, N_FFN1, range(4))
            act.wait_ge(start_step, ROPE_STEPS)
            act.activation(sin_sb[:, :, :], turns[:, :, :], ACT.Sin).then_inc(trig, 1)
            act.activation(cos_sb[:, :, :], turns_c[:, :, :], ACT.Sin).then_inc(trig, 1)
            with act.Fori(0, DEPTH) as layer:
                act.wait_ge(h_ready, layer * NORM_PIECES + 4)
                act.dma_start(gate_bias[:, :], b_gates[bass.ds(layer, 1), :, :].rearrange("a g d -> (a g d)")
                              .partition_broadcast(P)).then_inc(bias_landed, 16)
                norm_his(layer, N_FFN1, (2,))
                split_hi(FFN1 + 2, layer)
                norm_his(layer, N_FFN1, (3,))
                ffn(layer, FFN1, N_FFN1, M_FFN1, T_FFN1)
                norm_his(layer, N_MIX, (0, 1))
                split_hi(WIN + 2, layer)
                norm_his(layer, N_MIX, (2, 3))
                squares(layer, N_MIX)
                for u in range(WIN_UNITS):
                    if u == 1:
                        act.wait_ge(rstd_ready, layer * 4 + N_MIX + 1)
                    if u and not U_GATE < u <= U_QK:
                        win_unit(layer, u - 1)
                    if u == U_QK + 2:
                        act.preload_act_table(ACT.Silu)
                    if u == 19:
                        head_squares(layer, 0)
                    if u:
                        split_hi(ahead(WIN + 2 * u), layer)
                    if U_GATE < u <= U_QK:
                        win_unit(layer, u - 1)
                    if u == 19:
                        head_his(layer, 0)
                    split_hi(ahead(WIN + 2 * u + 1), layer)
                win_unit(layer, WIN_UNITS - 1)
                for hd in range(HEADS):
                    if hd == 3:
                        for i in range(2):
                            act.wait_ge(normed, layer * 2 + i + 1)
                            for k in range(4 * i, 4 * i + 4):
                                a = act.activation(yT[:, k, :], yT[:, k, :], ACT.Silu, bias=vec[:, V_LNB, k:k + 1],
                                                   scale=vec[:, V_LNG, k:k + 1])
                            a.then_inc(ln_silu, 1)
                            act.wait_ge(ln_silu, layer * 2 + i + 1)
                            act.activation(uT_hi[:, 4 * i:4 * i + 4, :], yT[:, 4 * i:4 * i + 4, :], ACT.Copy
                                           ).then_inc(ln_hi, 1)
                    if hd == 2:
                        act.wait_ge(mean_done, layer * 2 + 2)
                        act.activation(channel_std, ps[:, T1, 0:SEQ], ACT.Sqrt, bias=eps_tile[:, 0:1]
                                       ).then_inc(std_ready, 1)
                        act.preload_act_table(ACT.Silu)
                    split_hi(ahead(RET + 2 * hd), layer)
                    if hd + 1 < HEADS:
                        head_squares(layer, hd + 1)
                    if hd == 0:
                        act.wait_ge(mean_done, layer * 2 + 1)
                        act.activation(channel_mean, ps[:, T1, 0:SEQ], ACT.Copy).then_inc(mean_copied, 1)
                    split_hi(ahead(RET + 2 * hd + 1), layer)
                    if hd + 1 < HEADS:
                        head_his(layer, hd + 1)
                    if hd == 0:
                        for i in range(2):
                            act.wait_ge(centred, layer * 2 + i + 1)
                            act.activation(centred_sq[:, 4 * i:4 * i + 4, :], yT[:, 4 * i:4 * i + 4, :], ACT.Square
                                           ).then_inc(squared, 1)
                    if hd == 1:
                        act.preload_act_table(ACT.Sqrt)
                split_hi(CONVO + 2, layer)
                split_hi(CONVO + 3, layer)
                act.wait_ge(convT_lo, layer * 4 + 4)
                act.dma_start(p_in[:, :, :], p[bass.ds(layer, 1), :, :, :].rearrange("a b (t p) d -> p (a b t) d", p=P)
                              ).then_inc(p_landed, 16)
                act.wait_ge(score_done, layer * HEADS + HEADS)
                act.dma_start(gain_e[:, :], ple_gain[bass.ds(layer, 1), :].rearrange("a d -> (a d)")
                              .partition_broadcast(P)).then_inc(gain_landed, 16)
                act.dma_start(gain_f[:, :], final_gain.partition_broadcast(P)).then_inc(gain_landed, 16)
                split_hi(OUT, layer)
                m_his(layer, (0, 1))
                split_hi(OUT + 1, layer)
                split_hi(OUT + 2, layer)
                m_his(layer, (2, 3))
                split_hi(OUT + 3, layer)
                act.wait_ge(p_T, layer + 1)
                act.activation(hT_hi[:, 0:2, :], ps[:, T0, :].rearrange("p (k t) -> p k t", k=2), ACT.Copy
                               ).then_inc(p_hi, 1)
                split_hi(FFN2 - 1, layer)
                norm_his(layer, N_FFN2, (0, 1))
                split_hi(FFN2, layer)
                split_hi(PLEP, layer)
                norm_his(layer, N_FFN2, (2, 3))
                squares(layer, N_FFN2)
                split_hi(FFN2 + 2, layer)
                act.wait_ge(norm_g, layer * NORM_PIECES + N_FFN2 * 4 + 4)
                act.dma_start(vec[:, :, :], vectors[:, bass.ds((layer + 1) * NVEC, NVEC), :]).then_inc(vec_landed, 16)
                act.dma_start(vec_ple[:, :], vectors[:, bass.ds(layer * NVEC + V_PLE, 1), :]
                              .rearrange("p a k -> p (a k)")).then_inc(ple_landed, 16)
                ffn(layer, FFN2, N_FFN2, M_FFN2, T_FFN2)
                norm_his(layer, N_PLE, (0, 1))
                split_hi(PG + 2, layer)
                norm_his(layer, N_PLE, (2, 3))
                squares(layer, N_PLE)
                split_hi(PG + 3, layer)
                with act.If(DEPTH - 1 - layer):
                    split_hi(LAYER, layer)
                act.wait_ge(rstd_ready, layer * 4 + N_PLE + 1)
                for n in range(2):
                    if n:
                        squares(layer + 1, N_FFN1, (0, 1))
                        with act.If(DEPTH - 1 - layer):
                            split_hi(LAYER + 1, layer)
                            norm_his(layer + 1, N_FFN1, (0, 1))
                    for t in range(TB):
                        unit_block(act, layer, t, T_PG + n, PG + 2 * n + 1)
                        act.activation(gate_b[:, t, cols(n)], ps[:, (4, 0)[n] + t, :], ACT.Sigmoid,
                                       scale=rstd[:, t:t + 1]).then_inc(pg_act, 1)
                act.preload_act_table(ACT.Silu)
                squares(layer + 1, N_FFN1, (2, 3))

        @block.vector
        def _(dve):
            def split_lo(c, layer, j=0):
                s = slot(c)
                dve.wait_ge(hi_done[s], nth(c, layer, j) + 1)
                dve.tensor_tensor(w_lo[:, s, :], raw[:, s, :], w_hi[:, s, :].bitcast(F32), ALU.subtract
                                  ).then_inc(lo_done[s], 1)

            def gains(layer, q, pieces):
                g = vec_ple if q == N_PLE else vec[:, (V_FFN1, V_MIX, V_FFN2)[q], :]
                for i in pieces:
                    n, t = half_of(i)
                    dve.wait_ge(norm_T, layer * NORM_PIECES + q * 4 + i + 1)
                    if i >= 2:
                        dve.wait_ge(norm_lo, layer * NORM_PIECES + q * 4 + i - 1)
                    dve.tensor_tensor(scaled[:, i % 2, :].rearrange("p (k t) -> p k t", k=4),
                                      ps[:, T0 + i % 2, :].rearrange("p (k t) -> p k t", k=4),
                                      g[:, 4 * n:4 * n + 4].unsqueeze(2).to_broadcast([P, 4, P]), ALU.mult
                                      ).then_inc(norm_g, 1)

            def norm_los(layer, q, pieces):
                for i in pieces:
                    n, t = half_of(i)
                    dve.wait_ge(norm_hi, layer * NORM_PIECES + q * 4 + i + 1)
                    dve.tensor_tensor(uT_lo[:, 4 * n:4 * n + 4, toks(t)],
                                      scaled[:, i % 2, :].rearrange("p (k t) -> p k t", k=4),
                                      uT_hi[:, 4 * n:4 * n + 4, toks(t)].bitcast(F32), ALU.subtract
                                      ).then_inc(norm_lo, 1)

            def gated_product(layer, n, bank, j=0):
                for t in range(TB):
                    dve.wait_ge(acted_ready, layer * 2 * MIDS + 2 * (n + j) + t + 1)
                    dve.scalar_tensor_tensor(mid[:, t, :], ps[:, bank + t, 256:512], rstd[:, t:t + 1], acted[:, t, :],
                                             ALU.mult, ALU.mult).then_inc(mid_ready, 1)

            def ffn(layer, F, mids):
                def mid_lower(k, to=0):
                    dve.wait_ge(mid_hi, layer * MIDS + mids + k + 1)
                    dve.tensor_tensor(hT_lo[:, to:to + 2, :], ps[:, T0, :].rearrange("p (k t) -> p k t", k=2),
                                      hT_hi[:, to:to + 2, :].bitcast(F32), ALU.subtract).then_inc(mid_lo, 1)

                split_lo(F + 2, layer)
                gated_product(layer, mids, 4 if F else 2)
                split_lo(F + 3, layer)

                def unit(j):
                    mid_lower(j)
                    split_lo(F + 4, layer, j)
                    split_lo(F + 5, layer, j)
                    gated_product(layer, mids + 1, 4, j)
                    split_lo(F + 6, layer, j)

                unit(0)
                if F:
                    dve.wait_ge(e_r, layer + 1)
                    dve.wait_ge(gain_landed, 32 * layer + 32)
                    for t in range(TB):
                        dve.scalar_tensor_tensor(e_buf[:, t, :], e_buf[:, t, :], r_e[:, t:t + 1], gain_e[:, :],
                                                 ALU.mult, ALU.mult).then_inc(e_normed, 1)
                with dve.Fori(1, FFN_UNITS - 1) as j:
                    unit(j)
                mid_lower(FFN_UNITS - 1, 2)

            def ffn_residual(layer, F, i):
                n, t = half_of(i)
                last_piece(dve, layer, i, P_FFN2 if F else P_FFN1, F + FFN_CHUNKS - 1)
                dve.scalar_tensor_tensor(h[:, t, cols(n)], ps[:, i, :], 0.5, h[:, t, cols(n)], ALU.mult, ALU.add
                                         ).then_inc(h_ready, 1)

            def after_ffn(layer, F, q):
                ffn_residual(layer, F, 0)
                ffn_residual(layer, F, 1)
                gains(layer, q, (0,))
                ffn_residual(layer, F, 2)
                norm_los(layer, q, (0,))
                gains(layer, q, (1,))
                ffn_residual(layer, F, 3)
                norm_los(layer, q, (1,))
                for i in (2, 3):
                    gains(layer, q, (i,))
                    norm_los(layer, q, (i,))

            def conv_taps(layer):
                dve.wait_ge(mid_hi, layer * MIDS + M_FFN2)
                dve.wait_ge(padded, layer + 1)
                for m in range(CONV_K * KT):
                    tap, k = m // KT, m % KT
                    src = gluT[:, k, tap:tap + SEQ]
                    weight = vec[:, V_TAPS + tap, k:k + 1]
                    if tap == 0:
                        op = dve.tensor_scalar(yT[:, k, :], src, weight, vec[:, V_CONVB, k:k + 1], ALU.mult, ALU.add)
                    else:
                        dve.wait_ge(conv_step, layer * CONV_K * KT + m - KT + 1)
                        op = dve.scalar_tensor_tensor(yT[:, k, :], src, weight, yT[:, k, :], ALU.mult, ALU.add)
                    op.then_inc(conv_step, 1)
                    yield

            def win_unit(layer, w):
                bank, last = w % 3 * 2, WIN + 2 * w + 1
                if w < U_GATE:
                    if w:
                        dve.wait_ge(mid_T, layer * MIDS + M_GLU + w)
                    gated_product(layer, M_GLU + w, bank)
                elif w < U_QK:
                    g = w - U_GATE
                    dest = gate_a if g < 2 else gate_b
                    if g == 0:
                        dve.wait_ge(bias_landed, 16 * layer + 16)
                    for t in range(TB):
                        unit_block(dve, layer, t, T_WIN + w, last)
                        dve.scalar_tensor_tensor(dest[:, t, cols(g % 2)], ps[:, bank + t, :], rstd[:, t:t + 1],
                                                 gate_bias[:, cols(g)], ALU.mult, ALU.add).then_inc(gate_pre, 1)

            def decay_scores(layer, hd):
                dve.wait_ge(score_done, layer * HEADS + hd + 1)
                dve.wait_ge(consts_late, 32)
                bank = 4 if hd else T0
                dve.tensor_tensor(scores[:, 0:SEQ], ps[:, bank, 0:SEQ], decay_sb[:, hd, :], ALU.mult)
                dve.tensor_tensor(scores[:, SEQ:3 * P], ps[:, bank, SEQ:3 * P], decay_sb[:, hd, 0:P], ALU.mult
                                  ).then_inc(decayed, 1)

            def head_outputs(layer, hd):
                dve.wait_ge(head_r, layer * HEADS + hd + 1)
                dve.wait_ge(unit_act, layer * UNIT_ACTS + 2 * (U_G - U_QK + hd) + 2)
                for t in range(TB):
                    dve.scalar_tensor_tensor(scaled[:, t, :], ps[:, 4 + t, :], r_head[:, t:t + 1],
                                             swish_g[:, t, hd * DV:(hd + 1) * DV], ALU.mult, ALU.mult
                                             ).then_inc(head_ready, 1)

            def head_los(layer, hd):
                for t in range(TB):
                    dve.wait_ge(head_hi, layer * 8 + 2 * hd + t + 1)
                    hi, lo = head_T_parts[hd % 2]
                    dve.tensor_tensor(lo[:, :, toks(t)], ps[:, T1 - t, :].rearrange("p (k t) -> p k t", k=4),
                                      hi[:, :, toks(t)].bitcast(F32), ALU.subtract).then_inc(head_lo, 1)

            def m_los(layer, pieces):
                for i in pieces:
                    n, t = half_of(i)
                    dve.wait_ge(m_hi, layer * 4 + i + 1)
                    dve.tensor_tensor(mT_lo[:, 4 * n:4 * n + 4, toks(t)],
                                      ps[:, T0 + i % 2, :].rearrange("p (k t) -> p k t", k=4),
                                      mT_hi[:, 4 * n:4 * n + 4, toks(t)].bitcast(F32), ALU.subtract
                                      ).then_inc(m_lo, 1)

            def conv_branch(layer, n):
                for t in range(TB):
                    unit_block(dve, layer, t, T_CONVO + n, CONVO + 2 * n + 1)
                    dve.wait_ge(gate_act, layer * 4 + n + 1)
                    dve.tensor_tensor(gate_a[:, t, cols(n)], ps[:, (4, 0)[n] + t, :], gate_a[:, t, cols(n)], ALU.mult
                                      ).then_inc(conv_gated, 1)
                for t in range(TB):
                    dve.wait_ge(conv_gated, layer * 4 + 2 * n + t + 1)
                    dve.tensor_tensor(gate_a[:, t, cols(n)], gate_a[:, t, cols(n)], gate_b[:, t, cols(n)], ALU.add
                                      ).then_inc(m_ready, 1)

            done = [0]

            def step(op):
                done[0] += 1
                op.then_inc(start_step, 1)
                dve.wait_ge(start_step, done[0])

            for s in range(SLOTS):
                dve.sem_inc(lo_done[s], 1)
            dve.wait_ge(rope_in, 32)
            step(dve.tensor_copy(pos_f[:, :], pos_i[:, :]))
            for t in range(TB):
                step(dve.tensor_scalar(angle[:, t, :], inv_sb[:, :], pos_f[:, t:t + 1], None, ALU.mult))
            step(dve.tensor_scalar(turns[:, :, :], angle[:, :, :], 1.0 / TWO_PI, MAGIC, ALU.mult, ALU.add))
            step(dve.tensor_scalar(turns_c[:, :, :], angle[:, :, :], 1.0 / TWO_PI, 0.25, ALU.mult, ALU.add))
            step(dve.tensor_scalar(turns[:, :, :], turns[:, :, :], -MAGIC, None, ALU.add))
            step(dve.tensor_scalar(turns_c[:, :, :], turns_c[:, :, :], MAGIC, -MAGIC, ALU.add, ALU.add))
            for buf, keep in ((turns, 0), (turns_c, 1)):
                src = angle[:, :, :]
                for n, c in enumerate((C1, C2, C3)):
                    acc = junk[:, keep * 256:keep * 256 + 256].rearrange("p (t f) -> p t f", t=TB)
                    step(dve.scalar_tensor_tensor(acc, buf[:, :, :], -c, src, ALU.mult, ALU.add))
                    src = acc
                step(dve.tensor_scalar(acc, acc, TWO_PI / 4 if keep else 0.0, PI_IN, ALU.add, ALU.min))
                step(dve.tensor_scalar(buf[:, :, :], acc, -PI_IN, None, ALU.max))
            assert done[0] == ROPE_STEPS, done[0]
            dve.wait_ge(vec_landed, 16)
            gains(0, N_FFN1, (0,))
            split_lo(0, 0)
            norm_los(0, N_FFN1, (0,))
            gains(0, N_FFN1, (1,))
            norm_los(0, N_FFN1, (1,))
            with dve.Fori(0, DEPTH) as layer:
                for i in (2, 3):
                    gains(layer, N_FFN1, (i,))
                    norm_los(layer, N_FFN1, (i,))
                ffn(layer, FFN1, M_FFN1)
                after_ffn(layer, FFN1, N_MIX)
                taps = None
                for u in range(WIN_UNITS):
                    if u:
                        win_unit(layer, u - 1)
                    if u == 18:
                        decay_scores(layer, 0)
                    if u == 19:
                        head_outputs(layer, 0)
                    if u == CONV_UNIT:
                        taps = conv_taps(layer)
                    for half, c in enumerate((ahead(WIN + 2 * u), ahead(WIN + 2 * u + 1))):
                        if c not in POOL_SPLITS:
                            split_lo(c, layer)
                        for _ in range(conv_steps(u, half)):
                            next(taps, None)
                        if u == 19 and not half:
                            head_los(layer, 0)
                            decay_scores(layer, 1)

                def normalised(i):
                    part = yT[:, 4 * i:4 * i + 4, :]
                    dve.tensor_tensor(part, part, channel_std.unsqueeze(1).to_broadcast([P, 4, SEQ]), ALU.mult
                                      ).then_inc(normed, 1)

                for hd in range(HEADS):
                    if hd == 3:
                        for n in range(2):
                            dve.wait_ge(ln_hi, layer * 2 + n + 1)
                            for t in range(TB):
                                part = (slice(None), slice(4 * n, 4 * n + 4), toks(t))
                                dve.tensor_tensor(uT_lo[part], yT[part], uT_hi[part].bitcast(F32), ALU.subtract
                                                  ).then_inc(convT_lo, 1)
                    split_lo(ahead(RET + 2 * hd), layer)
                    if hd == 2:
                        dve.wait_ge(std_ready, layer + 1)
                        dve.reciprocal(channel_std, channel_std).then_inc(ln_rstd, 1)
                        dve.wait_ge(ln_rstd, layer + 1)
                        normalised(0)
                    if hd + 1 < HEADS:
                        head_outputs(layer, hd + 1)
                    if hd == 2:
                        normalised(1)
                    if hd == 0:
                        dve.wait_ge(mean_copied, layer + 1)
                        for i in range(2):
                            part = yT[:, 4 * i:4 * i + 4, :]
                            dve.tensor_tensor(part, part, channel_mean.unsqueeze(1).to_broadcast([P, 4, SEQ]),
                                              ALU.subtract).then_inc(centred, 1)
                    if hd + 1 < HEADS:
                        head_los(layer, hd + 1)
                    if hd + 2 < HEADS:
                        decay_scores(layer, hd + 2)
                    split_lo(ahead(RET + 2 * hd + 1), layer)
                for i in range(4):
                    n, t = half_of(i)
                    last_piece(dve, layer, i, P_RET, RET + 7)
                    dve.wait_ge(gate_act, layer * 4 + n + 3)
                    dve.tensor_tensor(gate_b[:, t, cols(n)], ps[:, i, :], gate_b[:, t, cols(n)], ALU.mult
                                      ).then_inc(ret_gated, 1)
                split_lo(CONVO + 2, layer)
                split_lo(CONVO + 3, layer)
                conv_branch(layer, 0)
                split_lo(OUT, layer)
                m_los(layer, (0, 1))
                split_lo(OUT + 1, layer)
                conv_branch(layer, 1)
                split_lo(OUT + 2, layer)
                m_los(layer, (2, 3))
                split_lo(OUT + 3, layer)

                def out_residual(n):
                    for t in range(TB):
                        unit_block(dve, layer, t, T_OUT + n, OUT + 2 * n + 1)
                        dve.tensor_tensor(h[:, t, cols(n)], ps[:, (2, 0)[n] + t, :], h[:, t, cols(n)], ALU.add
                                          ).then_inc(h_ready, 1)

                out_residual(0)
                dve.wait_ge(p_hi, layer + 1)
                dve.tensor_tensor(hT_lo[:, 0:2, :], ps[:, T0, :].rearrange("p (k t) -> p k t", k=2),
                                  hT_hi[:, 0:2, :].bitcast(F32), ALU.subtract).then_inc(p_lo, 1)
                split_lo(FFN2 - 1, layer)
                gains(layer, N_FFN2, (0, 1))
                norm_los(layer, N_FFN2, (0, 1))
                split_lo(FFN2, layer)
                out_residual(1)
                for i in (2, 3):
                    gains(layer, N_FFN2, (i,))
                    norm_los(layer, N_FFN2, (i,))
                split_lo(PLEP, layer)
                ffn(layer, FFN2, M_FFN2)
                dve.wait_ge(ple_landed, 16 * layer + 16)
                after_ffn(layer, FFN2, N_PLE)
                split_lo(PG + 2, layer)
                split_lo(PG + 3, layer)
                with dve.If(DEPTH - 1 - layer):
                    split_lo(LAYER, layer)
                dve.wait_ge(e_normed, layer * TB + TB)
                for n in range(2):
                    for t in range(TB):
                        dve.wait_ge(pg_act, layer * 4 + 2 * n + t + 1)
                        dve.tensor_tensor(gate_b[:, t, cols(n)], gate_b[:, t, cols(n)], e_buf[:, t, cols(n)], ALU.mult
                                          ).then_inc(pg_prod, 1)
                        dve.wait_ge(pg_prod, layer * 4 + 2 * n + t + 1)
                        dve.tensor_tensor(h[:, t, cols(n)], h[:, t, cols(n)], gate_b[:, t, cols(n)], ALU.add
                                          ).then_inc(h_ready, 1)
                    if n == 0:
                        with dve.If(DEPTH - 1 - layer):
                            dve.wait_ge(vec_landed, 16 * layer + 32)
                            gains(layer + 1, N_FFN1, (0, 1))
                            norm_los(layer + 1, N_FFN1, (0, 1))
            for t in range(TB):
                dve.wait_ge(rstd_ready, DEPTH * 4 + t + 1)
                for n in range(2):
                    dve.scalar_tensor_tensor(e_buf[:, t, cols(n)], h[:, t, cols(n)], rstd[:, t:t + 1],
                                             gain_f[:, cols(n)], ALU.mult, ALU.mult).then_inc(out_ready, 1)

        @block.gpsimd
        def _(pool):
            def split_lo(c, layer):
                s = slot(c)
                pool.wait_ge(hi_done[s], nth(c, layer) + 1)
                pool.tensor_tensor(w_lo[:, s, :], raw[:, s, :], w_hi[:, s, :].bitcast(F32), ALU.subtract
                                   ).then_inc(lo_done[s], 1)

            def inverse_root(mean, with_eps, result, steps):
                pool.tensor_tensor(with_eps, mean, eps_tile, ALU.add).then_inc(pool_step, 1)
                pool.wait_ge(pool_step, steps + 1)
                return pool.tensor_tensor(result, with_eps, minus_half, ALU.pow)

            def norm_rstd(layer, q, steps):
                pool.wait_ge(ssq_ready, layer * NORM_PIECES + q * 4 + 4)
                pool.tensor_tensor(ssq_sum, ssq[:, :, 0], ssq[:, :, 1], ALU.add).then_inc(pool_step, 1)
                pool.wait_ge(pool_step, steps + 1)
                inverse_root(ssq_sum, ms, rstd, steps + 1).then_inc(rstd_ready, 1)

            def sum_tiles(layer, src, steps):
                for n in (4, 2, 1):
                    pool.tensor_tensor(centred_sq[:, 0:n, :], src[:, 0:n, :], src[:, n:2 * n, :], ALU.add
                                       ).then_inc(tile_sum, 1)
                    steps += 1
                    pool.wait_ge(tile_sum, layer * 6 + steps)
                    src = centred_sq

            pool.memset(minus_half, -0.5).then_inc(preset, 1)
            pool.memset(eps_tile, EPS).then_inc(preset, 1)
            pool.memset(zero, 0.0).then_inc(preset, 1)
            pool.wait_ge(preset, 3)
            zeros = zero.unsqueeze(1).to_broadcast([P, KT, PAD])
            split_lo(1, 0)
            pool.wait_ge(trig, 2)
            with pool.Fori(0, DEPTH) as layer:
                steps = layer * POOL_STEPS
                pool.wait_ge(h_ready, layer * NORM_PIECES + 4)
                pool.tensor_tensor(gluT[:, :, 0:PAD], zeros, zeros, ALU.add).then_inc(padded, 1)
                norm_rstd(layer, N_FFN1, steps)
                split_lo(WIN + 1, layer)
                norm_rstd(layer, N_MIX, steps + 2)
                for c in POOL_SPLITS[:4]:
                    split_lo(c, layer)
                pool.wait_ge(gate_pre, layer * 8 + 8)
                for w in range(4):
                    pool.wait_ge(unit_act, layer * UNIT_ACTS + 2 * w + 2)
                    if w:
                        pool.wait_ge(qk_T, layer * 8 + 2 * w)
                    z = qk_in[:, w % 2]
                    t1, t2 = z[:, :, :, 0, :], z[:, :, :, 1, :]
                    cos = cos_sb[:, :, :].unsqueeze(2).to_broadcast([P, TB, 2, HALF])
                    sin = sin_sb[:, :, :].unsqueeze(2).to_broadcast([P, TB, 2, HALF])
                    pa, pb = prod_a[:, :, :, :], prod_b[:, :, :, :]
                    last = layer * 20 + 5 * w
                    pool.tensor_tensor(pa, t1, cos, ALU.mult).then_inc(rope_step, 1)
                    pool.tensor_tensor(pb, t2, sin, ALU.mult).then_inc(rope_step, 1)
                    pool.wait_ge(rope_step, last + 2)
                    pool.tensor_tensor(roped[:, :, :, 0, :], pa, pb, ALU.subtract).then_inc(rope_step, 1)
                    pool.wait_ge(rope_step, last + 3)
                    pool.tensor_tensor(pa, t2, cos, ALU.mult).then_inc(rope_step, 1)
                    pool.tensor_tensor(pb, t1, sin, ALU.mult).then_inc(rope_step, 1)
                    pool.wait_ge(rope_step, last + 5)
                    pool.tensor_tensor(roped[:, :, :, 1, :], pa, pb, ALU.add).then_inc(roped_ready, 1)
                for c in POOL_SPLITS[4:]:
                    split_lo(c, layer)
                for hd in range(HEADS):
                    if hd == 1:
                        pool.wait_ge(conv_step, (layer + 1) * CONV_K * KT)
                        pool.wait_ge(used[slot(RET - 2)], nth(RET - 2, layer) + 2)
                        sum_tiles(layer, yT, 0)
                    if hd == 2:
                        pool.wait_ge(squared, layer * 2 + 2)
                        sum_tiles(layer, centred_sq, 3)
                    pool.wait_ge(head_ssq, layer * 8 + 2 * hd + 2)
                    inverse_root(ssq_head, ms_head, r_head, steps + 4 + hd).then_inc(head_r, 1)
                norm_rstd(layer, N_FFN2, steps + 8)
                pool.wait_ge(e_squared, layer * 4 + 4)
                pool.tensor_tensor(ssq_e_sum, ssq_e[:, :, 0], ssq_e[:, :, 1], ALU.add).then_inc(pool_step, 1)
                pool.wait_ge(pool_step, steps + 11)
                inverse_root(ssq_e_sum, ms_e, r_e, steps + 11).then_inc(e_r, 1)
                split_lo(PG + 1, layer)
                norm_rstd(layer, N_PLE, steps + 12)
                with pool.If(DEPTH - 1 - layer):
                    split_lo(LAYER + 1, layer)
            for t in range(TB):
                steps = DEPTH * POOL_STEPS + 2 * t
                pool.wait_ge(ssq_ready, DEPTH * NORM_PIECES + TB + t + 1)
                pool.tensor_tensor(ssq_sum[:, t:t + 1], ssq[:, t, 0:1], ssq[:, t, 1:2], ALU.add).then_inc(pool_step, 1)
                pool.wait_ge(pool_step, steps + 1)
                pool.tensor_tensor(ms[:, t:t + 1], ssq_sum[:, t:t + 1], eps_tile[:, 0:1], ALU.add).then_inc(pool_step, 1)
                pool.wait_ge(pool_step, steps + 2)
                pool.tensor_tensor(rstd[:, t:t + 1], ms[:, t:t + 1], minus_half[:, 0:1], ALU.pow).then_inc(rstd_ready, 1)


def columns_chunks(w):
    return w.reshape(2, 4, P, COLS).transpose(0, 2, 1, 3).reshape(2, P, CHUNK)


def rows_chunks(w):
    return w.reshape(-1, 2, P, D).transpose(0, 2, 1, 3).reshape(-1, P, CHUNK)


def layer_chunks(i, w):
    def ffn(gate, up, down):
        down = rows_chunks(down)
        parts = []
        for k in range(FFN_UNITS):
            c = slice(256 * k, 256 * (k + 1))
            parts.append(columns_chunks(np.concatenate([gate[:, c], up[:, c]], axis=1)))
            if k:
                parts.append(down[k - 1:k])
        return parts + [down[-1:]]

    def units(m):
        return [columns_chunks(m[:, COLS * n:COLS * (n + 1)]) for n in range(m.shape[1] // COLS)]

    w_in = w["w_in"][i]
    conv_a, conv_b, q, k, v, g, gate_a, gate_b = np.split(w_in, np.cumsum([D, D, D, D, 2 * D, 2 * D, D]), axis=1)
    parts = ffn(w["ffn1_w_gate"][i], w["ffn1_w_up"][i], w["ffn1_w_down"][i])
    for n in range(4):
        c = slice(256 * n, 256 * (n + 1))
        parts.append(columns_chunks(np.concatenate([conv_b[:, c], conv_a[:, c]], axis=1)))
    for m in (gate_a, gate_b, q, k, v, g):
        parts += units(m)
    parts.append(rows_chunks(w["w_ret_o"][i]))
    parts += units(w["w_conv_o"][i]) + units(w["w_out"][i])
    first, *rest = ffn(w["ffn2_w_gate"][i], w["ffn2_w_up"][i], w["ffn2_w_down"][i])
    parts += [first, rows_chunks(w["w_ple_proj"][i])] + rest
    parts += units(w["w_ple_gate"][i])
    return parts


def shape_constants():
    f = np.float32
    log_g = np.log1p(-np.exp2(f(-5.0) - np.arange(HEADS, dtype=f))).astype(f)
    rel = (np.arange(SEQ, dtype=f)[None, :] - np.arange(P, dtype=f)[:, None])
    decay = np.where(rel >= 0, np.exp(log_g[:, None, None] * np.maximum(rel, f(0)), dtype=f), f(0))
    decay = (decay * f(DK ** -0.5)).astype(f).transpose(1, 0, 2)
    inv = np.power(f(ROPE_BASE), -np.arange(HALF, dtype=f) / f(HALF)).astype(f)
    return {
        "decay": np.ascontiguousarray(decay),
        "inv_freq": np.ascontiguousarray(np.broadcast_to(inv, (P, HALF))),
        "identity": np.eye(P, dtype=f),
        "mean_matrix": np.full((P, P), 1.0 / D, dtype=f),
    }


def kernel(**inputs):
    import concourse.bacc as bacc
    from concourse.bass_utils import run_bass_kernel_spmd

    w = {name: np.asarray(a) for name, a in inputs.items()}
    parts = [c for i in range(DEPTH) for c in layer_chunks(i, w)]
    names = ["ffn1_norm", "mix_norm", "ffn2_norm", "ple_norm", "conv_b", "conv_ln_g", "conv_ln_b"]
    vectors = np.concatenate([np.stack([w[n] for n in names], axis=1), w["conv_w"]], axis=1)
    vectors = np.concatenate([vectors, vectors[:1]], axis=0)
    arrays = {
        "stream": np.concatenate(parts, axis=0),
        "x": w["x"], "p": w["p"], "positions": w["positions"].reshape(TB, P).T,
        "vectors": np.ascontiguousarray(vectors.reshape(-1, KT, P).transpose(2, 0, 1)),
        "b_gates": w["b_gates"], "ple_gain": w["ple_proj_norm"], "final_gain": w["final_norm"],
        **shape_constants(),
    }
    nc = bacc.Bacc("TRN2", target_bir_lowering=False, num_devices=1)
    arrays = {f"in_{n}": np.ascontiguousarray(a) for n, a in arrays.items()}
    args = [nc.dram_tensor(n, a.shape, mybir.dt.from_np(a.dtype), kind="ExternalInput").ap() for n, a in arrays.items()]
    out = nc.dram_tensor("out", (1, SEQ, D), F32, kind="ExternalOutput").ap()
    build_kernel(nc, *args, out)
    return run_bass_kernel_spmd(nc, [arrays], core_ids=[0]).results[0]["out"]
```
